# Optimizing a Trainium2 kernel written in Bass

```python
import jax
import jax.numpy as jnp
from jax import lax
import numpy as np

D_MODEL = 1024
BATCH = 1
SEQ = 256
DEPTH = 2

GRID_W = 64
CTX_LEN = 256
EPS = 1e-6
F32 = jnp.float32
A_HEADS = 4
A_DK = 128
A_DV = 128
A_WIDTH = A_HEADS * A_DK
A_VWIDTH = A_HEADS * A_DV
CHUNK = 64
B_HEADS = 8
B_KV_HEADS = 2
B_HD = 64
B_GROUP = B_HEADS // B_KV_HEADS
B_WIDTH = B_HEADS * B_HD
B_KV_WIDTH = B_KV_HEADS * B_HD
Q_BLOCK = 128
ROPE_THETA = 10000.0
AXIS_DIM = B_HD // 2
N_GROUPS = 4
EXPERTS_PER_GROUP = 8
N_EXPERTS = N_GROUPS * EXPERTS_PER_GROUP
TOP_K = 2
D_EXPERT = 512
ROW_BLOCK = 128
IN_SIZES = (A_WIDTH, A_WIDTH, A_WIDTH, A_VWIDTH, A_VWIDTH, B_WIDTH, B_KV_WIDTH, B_KV_WIDTH, D_MODEL, D_MODEL)
D_IN = A_WIDTH * 3 + A_VWIDTH * 2 + B_WIDTH + 2 * B_KV_WIDTH + 2 * D_MODEL
N_MOD = 6

kernel_name = 'hybrid_hgrn2_gqa_hier_moe_dit'

def rmsnorm(x, g):
    xf = x.astype(F32)
    y = xf * lax.rsqrt(jnp.mean(xf * xf, axis=-1, keepdims=True) + EPS)
    return (y * g.astype(F32)).astype(x.dtype)

def split_in(z):
    parts, off = [], 0
    for s in IN_SIZES:
        parts.append(z[..., off:off + s])
        off += s
    return parts

def to_heads(t, n_heads):
    bsz, n, w = t.shape
    return t.reshape(bsz, n, n_heads, w // n_heads).transpose(0, 2, 1, 3)

def from_heads(t):
    bsz, h, n, d = t.shape
    return t.transpose(0, 2, 1, 3).reshape(bsz, n, h * d)

def axial_rope_tables(rows):
    t = jnp.arange(rows * GRID_W)
    r = (t // GRID_W).astype(F32)
    col = (t % GRID_W).astype(F32)
    inv = ROPE_THETA ** (-jnp.arange(0, AXIS_DIM, 2, dtype=F32) / AXIS_DIM)
    ang = jnp.stack([r[:, None] * inv, col[:, None] * inv], axis=1)
    return jnp.cos(ang), jnp.sin(ang)

def apply_rope(x, cos, sin):
    shp = x.shape
    xa = x.astype(F32).reshape(shp[:-1] + (2, 2, AXIS_DIM // 2))
    x1, x2 = xa[..., 0, :], xa[..., 1, :]
    out = jnp.stack([x1 * cos - x2 * sin, x2 * cos + x1 * sin], axis=-2)
    return out.reshape(shp).astype(x.dtype)

def hgrn_gates(zf, lb):
    zf = zf.astype(F32)
    logf = jnp.logaddexp(jnp.log(lb), jnp.log1p(-lb) + jax.nn.log_sigmoid(zf))
    k = (1.0 - lb) * jax.nn.sigmoid(-zf)
    return k, logf

def gla_final_state(k, v, logf):
    b = jnp.cumsum(logf, axis=-2)
    return jnp.einsum('bhsk,bhsv->bhkv', k * jnp.exp(b[..., -1:, :] - b), v)

def gla_chunk_scan(q, k, v, logf, s0):
    bsz, h, n, _ = q.shape
    dv = v.shape[-1]
    nc = n // CHUNK

    def chunks(t):
        return jnp.moveaxis(t.reshape(bsz, h, nc, CHUNK, t.shape[-1]), 2, 0)

    lower = jnp.tril(jnp.ones((CHUNK, CHUNK), bool))[:, :, None]

    def step(state, inp):
        qc, kc, vc, lfc = inp
        b = jnp.cumsum(lfc, axis=-2)
        o_inter = jnp.einsum('bhtk,bhkv->bhtv', qc * jnp.exp(b), state)
        diff = b[..., :, None, :] - b[..., None, :, :]
        decay = jnp.exp(jnp.where(lower, diff, -jnp.inf))
        scores = jnp.einsum('bhtk,bhsk,bhtsk->bhts', qc, kc, decay)
        o_intra = jnp.einsum('bhts,bhsv->bhtv', scores, vc)
        b_last = b[..., -1:, :]
        new_state = jnp.exp(b_last[..., 0, :])[..., None] * state + jnp.einsum('bhsk,bhsv->bhkv', kc * jnp.exp(b_last - b), vc)
        return new_state, o_inter + o_intra

    _, o = lax.scan(step, s0, (chunks(q), chunks(k), chunks(v), chunks(logf)))
    return jnp.moveaxis(o, 0, 2).reshape(bsz, h, n, dv)

def gated_head_norm(o, gz, g):
    bsz, h, n, dv = o.shape
    o = o.transpose(0, 2, 1, 3)
    o = o * lax.rsqrt(jnp.mean(o * o, axis=-1, keepdims=True) + EPS) * g.astype(F32).reshape(h, dv)
    gate = jax.nn.silu(gz.astype(F32)).reshape(bsz, n, h, dv)
    return (o * gate).reshape(bsz, n, h * dv).astype(gz.dtype)

def hgrn2_mixer(parts_lat, parts_ctx, lb_fwd, lb_bwd, norm_g, need_ctx):
    def prep(qz, ffz, fbz, iz):
        q = jax.nn.silu(to_heads(qz, A_HEADS).astype(F32)) * (A_DK ** -0.5)
        v = to_heads(iz, A_HEADS).astype(F32)
        kf, lf = hgrn_gates(to_heads(ffz, A_HEADS), lb_fwd)
        kb, lbw = hgrn_gates(to_heads(fbz, A_HEADS), lb_bwd)
        return q, v, kf, lf, kb, lbw

    def flip(t):
        return jnp.flip(t, axis=-2)

    ql, vl, kfl, lfl, kbl, lbl = prep(*parts_lat[:4])
    qc, vc, kfc, lfc, kbc, lbc = prep(*parts_ctx[:4])
    s_fwd = gla_final_state(kfc, vc, lfc)
    s_bwd = gla_final_state(flip(kbc), flip(vc), flip(lbc))
    o_lat = gla_chunk_scan(ql, kfl, vl, lfl, s_fwd) + flip(gla_chunk_scan(flip(ql), flip(kbl), flip(vl), flip(lbl), s_bwd))
    out_lat = gated_head_norm(o_lat, parts_lat[4], norm_g)
    if not need_ctx:
        return out_lat, None
    zero = jnp.zeros_like(s_fwd)
    o_ctx = gla_chunk_scan(qc, kfc, vc, lfc, zero) + flip(gla_chunk_scan(flip(qc), flip(kbc), flip(vc), flip(lbc), zero))
    return out_lat, gated_head_norm(o_ctx, parts_ctx[4], norm_g)

def attend(q, k, v):
    s = jnp.einsum('bkgqd,bkld->bkgql', q, k).astype(F32) * (B_HD ** -0.5)
    p = jax.nn.softmax(s, axis=-1).astype(v.dtype)
    return jnp.einsum('bkgql,bkld->bkgqd', p, v)

def gqa_mixer(parts_lat, parts_ctx, q_norm_g, k_norm_g, cos, sin, need_ctx):
    def prep(qz, kz, vz):
        q = rmsnorm(to_heads(qz, B_HEADS), q_norm_g)
        k = rmsnorm(to_heads(kz, B_KV_HEADS), k_norm_g)
        v = to_heads(vz, B_KV_HEADS)
        return q, k, v

    ql, kl, vl = prep(*parts_lat[5:8])
    qc, kc, vc = prep(*parts_ctx[5:8])
    ql = apply_rope(ql, cos, sin)
    kl = apply_rope(kl, cos, sin)
    k_all = jnp.concatenate([kc, kl], axis=2)
    v_all = jnp.concatenate([vc, vl], axis=2)
    bsz, _, n, _ = ql.shape
    nb = n // Q_BLOCK
    qg = jnp.moveaxis(ql.reshape(bsz, B_KV_HEADS, B_GROUP, nb, Q_BLOCK, B_HD), 3, 0)
    o = lax.map(lambda qb: attend(qb, k_all, v_all), qg)
    o = jnp.moveaxis(o, 0, 3).reshape(bsz, B_HEADS, n, B_HD)
    out_lat = from_heads(o)
    if not need_ctx:
        return out_lat, None
    l = qc.shape[2]
    oc = attend(qc.reshape(bsz, B_KV_HEADS, B_GROUP, l, B_HD), kc, vc).reshape(bsz, B_HEADS, l, B_HD)
    return out_lat, from_heads(oc)

def hier_moe(xf, w_rg, b_rg, w_re, b_re, w_gate, w_up, w_down):
    t, d = xf.shape
    glog = (xf @ w_rg).astype(F32) + b_rg.astype(F32)
    gsel = jnp.argmax(glog, axis=-1)
    p_group = jnp.take_along_axis(jax.nn.softmax(glog, axis=-1), gsel[:, None], axis=1)[:, 0]
    elog_all = ((xf @ w_re).astype(F32) + b_re.astype(F32)).reshape(t, N_GROUPS, EXPERTS_PER_GROUP)
    elog = jnp.take_along_axis(elog_all, gsel[:, None, None], axis=1)[:, 0]
    top_p, top_i = lax.top_k(jax.nn.softmax(elog, axis=-1), TOP_K)
    weights = top_p / jnp.sum(top_p, axis=-1, keepdims=True) * p_group[:, None]
    expert_id = (gsel[:, None].astype(jnp.int32) * EXPERTS_PER_GROUP + top_i.astype(jnp.int32)).reshape(-1)
    m = t * TOP_K
    n_blocks = (m + ROW_BLOCK - 1) // ROW_BLOCK + N_EXPERTS
    r = n_blocks * ROW_BLOCK
    order = jnp.argsort(expert_id)
    e_sorted = expert_id[order]
    tok_sorted = (order // TOP_K).astype(jnp.int32)
    w_sorted = weights.reshape(-1)[order]
    counts = jnp.bincount(expert_id, length=N_EXPERTS)
    padded = (counts + ROW_BLOCK - 1) // ROW_BLOCK * ROW_BLOCK
    pad_end = jnp.cumsum(padded)
    start = jnp.cumsum(counts) - counts
    dest = (pad_end - padded)[e_sorted] + jnp.arange(m) - start[e_sorted]
    row_tok = jnp.full((r,), t, jnp.int32).at[dest].set(tok_sorted)
    row_w = jnp.zeros((r,), F32).at[dest].set(w_sorted)
    block_e = jnp.minimum(jnp.searchsorted(pad_end, jnp.arange(n_blocks) * ROW_BLOCK, side='right'), N_EXPERTS - 1)
    x_pad = jnp.concatenate([xf, jnp.zeros((1, d), xf.dtype)], axis=0)

    def expert_block(args):
        toks, wts, e = args
        xb = x_pad[toks]
        hb = jax.nn.silu(xb @ w_gate[e]) * (xb @ w_up[e])
        return (hb @ w_down[e]) * wts[:, None].astype(xf.dtype)

    yb = lax.map(expert_block, (row_tok.reshape(n_blocks, ROW_BLOCK), row_w.reshape(n_blocks, ROW_BLOCK), block_e))
    y = jax.ops.segment_sum(yb.reshape(r, d), row_tok, num_segments=t + 1)
    return y[:t]

def trunk_layer(h, hc, mod_lat, mod_ctx, cos, sin, norm1_g, norm2_g, w_in, lb_fwd, lb_bwd, hgrn_norm_g,
                q_norm_g, k_norm_g, w_up_a, w_up_b, w_out, w_rg, b_rg, w_re, b_re, w_gate, w_up, w_down, need_ctx):
    sh1, sc1, g1, sh2, sc2, g2 = jnp.split(mod_lat, N_MOD, axis=-1)
    csh1, csc1, cg1, csh2, csc2, cg2 = jnp.split(mod_ctx, N_MOD, axis=-1)
    xl = rmsnorm(h, norm1_g) * (1.0 + sc1) + sh1
    xc = rmsnorm(hc, norm1_g) * (1.0 + csc1) + csh1
    pl = split_in(xl @ w_in)
    pc = split_in(xc @ w_in)
    a_l, a_c = hgrn2_mixer(pl, pc, lb_fwd, lb_bwd, hgrn_norm_g, need_ctx)
    b_l, b_c = gqa_mixer(pl, pc, q_norm_g, k_norm_g, cos, sin, need_ctx)

    def merge(parts, ya, yb):
        return (jax.nn.sigmoid(parts[8]) * (ya @ w_up_a) + jax.nn.sigmoid(parts[9]) * (yb @ w_up_b)) @ w_out

    h = h + g1 * merge(pl, a_l, b_l)
    if need_ctx:
        hc = hc + cg1 * merge(pc, a_c, b_c)
    bsz, n, d = h.shape
    xl2 = rmsnorm(h, norm2_g) * (1.0 + sc2) + sh2
    if need_ctx:
        xc2 = rmsnorm(hc, norm2_g) * (1.0 + csc2) + csh2
        tokens = jnp.concatenate([xl2.reshape(-1, d), xc2.reshape(-1, d)], axis=0)
        y = hier_moe(tokens, w_rg, b_rg, w_re, b_re, w_gate, w_up, w_down)
        h = h + g2 * y[:bsz * n].reshape(bsz, n, d)
        hc = hc + cg2 * y[bsz * n:].reshape(hc.shape)
    else:
        y = hier_moe(xl2.reshape(-1, d), w_rg, b_rg, w_re, b_re, w_gate, w_up, w_down)
        h = h + g2 * y.reshape(bsz, n, d)
    return h, hc

def setup_inputs(seed: int = 0) -> dict:
    key = jax.random.key(seed)
    ks = jax.random.split(key, 24)

    def nrm(k, shape, scale):
        return jax.random.normal(k, shape, F32) * scale

    def gain(k, shape):
        return 1.0 + 0.05 * jax.random.normal(k, shape, F32)

    return {
        'x': nrm(ks[0], (BATCH, SEQ, D_MODEL), 1.0),
        'c': nrm(ks[1], (BATCH, D_MODEL), 1.0),
        'ctx': nrm(ks[2], (BATCH, CTX_LEN, D_MODEL), 1.0),
        'c_ctx': nrm(ks[3], (D_MODEL,), 1.0),
        'w_ada': nrm(ks[4], (DEPTH, D_MODEL, N_MOD * D_MODEL), 0.3 * D_MODEL ** -0.5),
        'b_ada': nrm(ks[5], (DEPTH, N_MOD * D_MODEL), 0.02),
        'norm1_g': gain(ks[6], (DEPTH, D_MODEL)),
        'norm2_g': gain(ks[7], (DEPTH, D_MODEL)),
        'w_in': nrm(ks[8], (DEPTH, D_MODEL, D_IN), D_MODEL ** -0.5),
        'lb_logits': nrm(ks[9], (2, DEPTH, A_WIDTH), 0.5),
        'hgrn_norm_g': gain(ks[10], (DEPTH, A_VWIDTH)),
        'q_norm_g': gain(ks[11], (DEPTH, B_HD)),
        'k_norm_g': gain(ks[12], (DEPTH, B_HD)),
        'w_up_a': nrm(ks[13], (DEPTH, A_VWIDTH, D_MODEL), A_VWIDTH ** -0.5),
        'w_up_b': nrm(ks[14], (DEPTH, B_WIDTH, D_MODEL), B_WIDTH ** -0.5),
        'w_out': nrm(ks[15], (DEPTH, D_MODEL, D_MODEL), D_MODEL ** -0.5),
        'w_router_group': nrm(ks[16], (DEPTH, D_MODEL, N_GROUPS), D_MODEL ** -0.5),
        'b_router_group': nrm(ks[17], (DEPTH, N_GROUPS), 0.01),
        'w_router_expert': nrm(ks[18], (DEPTH, D_MODEL, N_EXPERTS), D_MODEL ** -0.5),
        'b_router_expert': nrm(ks[19], (DEPTH, N_EXPERTS), 0.01),
        'w_gate': nrm(ks[20], (DEPTH, N_EXPERTS, D_MODEL, D_EXPERT), D_MODEL ** -0.5),
        'w_up': nrm(ks[21], (DEPTH, N_EXPERTS, D_MODEL, D_EXPERT), D_MODEL ** -0.5),
        'w_down': nrm(ks[22], (DEPTH, N_EXPERTS, D_EXPERT, D_MODEL), D_EXPERT ** -0.5),
        'final_norm_g': gain(ks[23], (D_MODEL,)),
    }

def reference(x, c, ctx, c_ctx, w_ada, b_ada, norm1_g, norm2_g, w_in, lb_logits, hgrn_norm_g, q_norm_g,
              k_norm_g, w_up_a, w_up_b, w_out, w_router_group, b_router_group, w_router_expert,
              b_router_expert, w_gate, w_up, w_down, final_norm_g):
    rows = x.shape[1] // GRID_W
    cos, sin = axial_rope_tables(rows)
    lb = jnp.cumsum(jax.nn.softmax(lb_logits.astype(F32), axis=1), axis=1)
    lb = lb - lb[:, :1]
    c_act = jax.nn.silu(c)
    cc_act = jax.nn.silu(c_ctx)
    h, hc = x, ctx
    for l in range(DEPTH):
        mod_lat = (c_act @ w_ada[l] + b_ada[l])[:, None, :]
        mod_ctx = cc_act @ w_ada[l] + b_ada[l]
        h, hc = trunk_layer(h, hc, mod_lat, mod_ctx, cos, sin, norm1_g[l], norm2_g[l], w_in[l],
                            lb[0, l].reshape(A_HEADS, 1, A_DK), lb[1, l].reshape(A_HEADS, 1, A_DK),
                            hgrn_norm_g[l], q_norm_g[l], k_norm_g[l], w_up_a[l], w_up_b[l], w_out[l],
                            w_router_group[l], b_router_group[l], w_router_expert[l], b_router_expert[l],
                            w_gate[l], w_up[l], w_down[l], l < DEPTH - 1)
    return rmsnorm(h, final_norm_g)


_drawn_inputs = setup_inputs


def setup_inputs(seed=0):
    import zlib

    import numpy as np

    out = dict(_drawn_inputs(seed))
    spreads = {}
    factors = {'ctx': 5.518,
     'c_ctx': 4.073,
     'b_ada': 2.995,
     'norm1_g': 7.001,
     'norm2_g': 3.302,
     'lb_logits': 8.0,
     'hgrn_norm_g': 7.77,
     'q_norm_g': 8.0,
     'k_norm_g': 8.0,
     'b_router_group': 25.55,
     'b_router_expert': 8.0}
    for name, (base, spread) in spreads.items():
        noise = np.random.default_rng([zlib.crc32(name.encode()), seed]).standard_normal(out[name].shape)
        drawn = base * np.exp(spread * noise) if base else spread * noise
        out[name] = jnp.asarray(drawn.astype(out[name].dtype))
    for name, factor in factors.items():
        out[name] = (out[name] * factor).astype(out[name].dtype)
    return out
```

```python
from contextlib import ExitStack

import numpy as np

import concourse.bass as bass
from concourse import mybir

F32 = mybir.dt.float32
I32 = mybir.dt.int32
U8 = mybir.dt.uint8
ALU = mybir.AluOpType
ACT = mybir.ActivationFunctionType
AX = mybir.AxisListType

P = 128
D = 1024
KD = D // P
DEPTH = 2
SEQ = 256
CTX = 256
NT = (SEQ + CTX) // P
LAT0 = CTX // P
EPS = 1e-6
HEADS = 4
AW = HEADS * P
B_HEADS, B_KV, HD = 8, 2, 64
GROUP = B_HEADS // B_KV
GRID_W = 64
AXIS = HD // 2
NG, EPG = 4, 8
NE = NG * EPG
DE = 512
CAP = 64
TOKENS = NT * P
RANK_STEPS = TOKENS // CAP
OVER = 2 * TOKENS // CAP
NB = NE + OVER
LEVELS = 7
BIG = 1e30
SLOT = KD * 512
KB = 256
MIX_SLOTS = 4
EXPERT_SLOTS = ((0, 1, 4), (2, 3, 5))
PAIRS = NE // 2
TINY = 2.0 ** -60

Q0, FF0, FB0, I0, GZ0 = 0, AW, 2 * AW, 3 * AW, 4 * AW
BQ0 = 5 * AW
BKV0 = BQ0 + B_HEADS * HD
Z80 = BKV0 + 2 * B_KV * HD
Z90 = Z80 + D
D_IN = Z90 + D

C_ID, C_UP, C_ONE, C_COS, C_SIN = 0, 128, 256, 384, 512
C_I64, C_INB, C_I32, C_REV, C_RG, C_TOK = 640, 704, 752, 784, 816, 820
C_N = 824


def float_constants():
    a = np.zeros((P, C_N), np.float32)
    a[:, C_ID:C_ID + P] = np.eye(P)
    a[:, C_UP:C_UP + P] = np.triu(np.ones((P, P)), 1)
    a[:, C_ONE:C_ONE + P] = 1.0
    t = np.arange(SEQ)
    inv = (np.float32(10000.0) ** (-np.arange(0, AXIS, 2, dtype=np.float32) / np.float32(AXIS))).astype(np.float32)
    pos = np.stack([(t // GRID_W), (t % GRID_W)], 1).astype(np.float32)
    ang = pos[:, :, None] * inv
    cos, sin = np.cos(ang), np.sin(ang)
    cc = np.stack([cos, cos], 2).reshape(SEQ, HD)
    ss = np.stack([-sin, sin], 2).reshape(SEQ, HD)
    for i in range(SEQ // P):
        a[:, C_COS + i * HD:C_COS + (i + 1) * HD] = cc[i * P:(i + 1) * P]
        a[:, C_SIN + i * HD:C_SIN + (i + 1) * HD] = ss[i * P:(i + 1) * P]
    a[:, C_I64:C_I64 + CAP] = np.arange(CAP)
    a[:, C_INB:C_INB + NB] = np.arange(NB)
    a[:, C_I32:C_I32 + NE] = np.arange(NE)
    a[:, C_REV:C_REV + NE] = NE - np.arange(NE)
    a[:, C_RG:C_RG + NG] = NG - np.arange(NG)
    a[:, C_TOK:C_TOK + NT] = np.arange(P)[:, None] + P * np.arange(NT) + 1
    return a


def level_masks():
    m = np.zeros((P, 2, LEVELS, P), np.float32)
    i = np.arange(P)
    for lv in range(LEVELS):
        half = P >> (lv + 1)
        same = (i[:, None] // (2 * half)) == (i[None, :] // (2 * half))
        second = (i // half) % 2 == 1
        fwd = same & ~second[:, None] & second[None, :]
        m[:, 0, lv] = fwd
        m[:, 1, lv] = fwd.T
    return m.reshape(P, 2 * LEVELS * P)


class Signal:

    def __init__(self, semaphore, first):
        self.sem, self.first = semaphore, first

    def at(self, layer, value):
        return self.sem, value + layer * self.first


class Family:

    def __init__(self, semaphores, before):
        self.semaphores, self.before = semaphores, before

    def sem(self, name):
        return self.semaphores[name]

    def at(self, name, value):
        return self.semaphores[name], value + self.before[name]


def plan_loads(layer):
    names = [(f"ada{n}", n % MIX_SLOTS) for n in range(12)]
    names += [(n, i % MIX_SLOTS) for i, n in enumerate(["ff", "fb", "q", "i", "gz", "bq", "bkv"])]
    names += [("up_a", 3), ("z8_0", 0), ("z8_1", 1), ("up_b", 2), ("z9_0", 0), ("z9_1", 1), ("out0", 3), ("out1", 2)]
    return names


def program(nc, x, c, ctx_in, c_ctx, w_ada, b_ada, norm1_g, norm2_g, w_in, lb_logits, hgrn_norm_g, q_norm_g,
            k_norm_g, w_up_a, w_up_b, w_out, w_rg, b_rg, w_re, b_re, w_gate, w_up, w_down, final_norm_g,
            consts, masks, out):
    mod_dram = nc.dram_tensor("mod_rows", (DEPTH, 2, 6 * D), F32, kind="Internal").ap()
    xs_dram = [nc.dram_tensor(f"moe_inputs_{L}", (TOKENS if L < DEPTH - 1 else SEQ, D), F32, kind="Internal").ap()
               for L in range(DEPTH)]
    y_dram = nc.dram_tensor("expert_outputs", (CAP, NB, D), F32, kind="Internal").ap()
    y_rows = y_dram.rearrange("c b d -> (c b) d")

    uses = [0] * 6
    where = [{} for _ in range(DEPTH)]
    expert_use = []
    tenant = [[None] * MIX_SLOTS for _ in range(DEPTH)]
    for L in range(DEPTH):
        for name, slot in plan_loads(L):
            where[L][name] = (slot, uses[slot], tenant[L][slot])
            uses[slot] += 1
            tenant[L][slot] = name
        expert_use.append(list(uses))
        for s in range(6):
            uses[s] += PAIRS

    with ExitStack() as ctx:
        def sb(name, shape, dt=F32):
            return ctx.enter_context(nc.sbuf_tensor(name, shape, dt))

        def sem(name):
            return ctx.enter_context(nc.semaphore(name))

        def sems(name):
            return [sem(f"{name}_{L}") for L in range(DEPTH)]

        ps = ctx.enter_context(nc.psum_tensor("ps", [P, 8, 512], F32))
        h = sb("h", [P, NT, D])
        xT = sb("xT", [P, KD, TOKENS])
        ring4 = sb("ring4", [P, MIX_SLOTS, SLOT])
        scr = sb("scr", [P, 104 * KB])
        cst = sb("cst", [P, C_N])
        msk = sb("msk", [P, 2, LEVELS, P], U8)
        stat = sb("stat", [P, 5, 4, NT])
        hst = sb("hst", [P, 4, 16])
        qst = sb("qst", [P, 4, NT * 10])
        mxs = sb("mxs", [P, 3, NT * B_HEADS])
        lbt = sb("lbt", [P, 10, 8])
        lbac = sb("lbac", [P, 2, 8])
        eb = sb("eb", [P, 2, 16])
        cin = sb("cin", [P, KD, 2])
        cact = sb("cact", [P, KD, 2])
        qkg = sb("qkg", [P, 2, HD])
        numi = sb("numi", [P, OVER + 1], I32)

        def area(k0, k1):
            return scr[:, int(k0 * KB):int(k1 * KB)]

        v = area(0, 8).rearrange("p (t n) -> p t n", t=NT)
        qf = area(8, 16).rearrange("p (h t) -> p h t", h=HEADS)
        cum = [area(16, 24).rearrange("p (h t) -> p h t", h=HEADS), area(24, 32).rearrange("p (h t) -> p h t", h=HEADS)]
        kg = [area(32, 40).rearrange("p (h t) -> p h t", h=HEADS), area(40, 48).rearrange("p (h t) -> p h t", h=HEADS)]
        amat = area(48, 56).rearrange("p (t h n) -> p t h n", t=NT, h=HEADS)
        zeros = area(48, 52)
        masks_in = area(56, 63)
        wlv = [area(56, 64).rearrange("p (h t) -> p h t", h=HEADS), area(64, 72).rearrange("p (h t) -> p h t", h=HEADS)]
        states = area(56, 68).rearrange("p (i h n) -> p i h n", i=6, h=HEADS)
        gz = area(72, 80).rearrange("p (t n) -> p t n", t=NT)
        bq = area(80, 88).rearrange("p (t n) -> p t n", t=NT)
        bkv = area(88, 92).rearrange("p (t n) -> p t n", t=NT)
        kT = area(92, 96).rearrange("p (h t) -> p h t", h=B_KV)
        kdn = area(96, 100).rearrange("p (b n) -> p b n", b=2)
        gbc = area(100, 104)
        qsq = area(100, 102)
        ng = area(102, 104)
        modR = area(12, 18).rearrange("p (n c) -> p n c", n=12)
        wr = area(8, 8 + KD * 36 / KB).rearrange("p (k n) -> p k n", k=KD)
        rb = area(9.25, 9.25 + 36 / KB)
        aT = area(8, 16).rearrange("p (k t) -> p k t", k=4)
        bT = area(0, 8).rearrange("p (k t) -> p k t", k=4)
        probs = area(24, 28).rearrange("p (b n) -> p b n", b=2)
        probsT = area(28, 32).rearrange("p (b n) -> p b n", b=2)
        qT = area(56, 72).rearrange("p (h t) -> p h t", h=B_HEADS)
        mT = area(32, 48).rearrange("p (k t) -> p k t", k=KD)
        sgm = area(96, 100).rearrange("p (b n) -> p b n", b=2)
        g1b = area(16, 24).rearrange("p (s n) -> p s n", s=2)
        ab = [area(32, 48).rearrange("p (s j n) -> p s j n", s=2, j=2), area(80, 96).rearrange("p (s j n) -> p s j n", s=2, j=2)]
        xn = [area(0, 8).rearrange("p (b n) -> p b n", b=2), area(24, 32).rearrange("p (b n) -> p b n", b=2)]
        junk = area(96, 100)
        ring45 = area(48, 80).rearrange("p (s n) -> p s n", s=2)
        xg = area(0, 8).rearrange("p (b n) -> p b n", b=2)
        yb = area(8, 12).rearrange("p (b n) -> p b n", b=2)
        g2b = area(16, 24).rearrange("p (s n) -> p s n", s=2)
        hid = area(44, 46).rearrange("p (b n) -> p b n", b=2)
        xgT = area(24, 28).rearrange("p (b k n) -> p b k n", b=2, k=KD)
        sg = area(28, 30).rearrange("p (b n) -> p b n", b=2)
        hT = area(30, 32).rearrange("p (b j n) -> p b j n", b=2, j=2)
        yg = area(80, 96).rearrange("p (b j n) -> p b j n", b=2, j=2)
        at = [32 * KB]

        def routing(n, dt=F32):
            a = scr[:, at[0]:at[0] + n]
            at[0] += n
            assert at[0] <= 44 * KB
            return a if dt is F32 else a.bitcast(dt)

        lg = routing(NT * 36).rearrange("p (t n) -> p t n", t=NT)
        grp = routing(NT * 4 * 4).rearrange("p (j t n) -> p j t n", j=4, t=NT)
        one = routing(NT * 12).rearrange("p (j t) -> p j t", j=12)
        em = routing(NT * NE).rearrange("p (t n) -> p t n", t=NT)
        em2 = routing(NT * NE).rearrange("p (t n) -> p t n", t=NT)
        oh = routing(2 * NT * NE).rearrange("p (j t n) -> p j t n", j=2, t=NT)
        tmpe = routing(NT * NE).rearrange("p (t n) -> p t n", t=NT)
        both = routing(NT * NE).rearrange("p (t n) -> p t n", t=NT)
        rank = routing(NT * NE).rearrange("p (t n) -> p t n", t=NT)
        nbk = routing(NT * NE).rearrange("p (t n) -> p t n", t=NT)
        cnt = routing(4 * NE).rearrange("p (j n) -> p j n", j=4)
        rowblk = routing(2 * 2 * NT).rearrange("p (j c t) -> p j c t", j=2, c=2)
        slotf = routing(2 * NT).rearrange("p (c t) -> p c t", c=2)
        tokslot = routing(2 * NT, I32).rearrange("p (c t) -> p c t", c=2)
        ohrow = routing(2 * NT * CAP).rearrange("p (j n) -> p j n", j=2 * NT)
        ohblk = routing(2 * NT * NB).rearrange("p (j n) -> p j n", j=2 * NT)
        idxf = routing(2 * NB).rearrange("p (j n) -> p j n", j=2)
        idx = routing(NB, I32)
        idxc = routing(2, I32)
        ovf = routing(OVER * NE).rearrange("p (j n) -> p j n", j=OVER)
        ovn = routing(OVER + 1)
        ident = cst[:, C_ID:C_ID + P]
        ones = cst[:, C_ONE:C_ONE + P]

        def slot_ap(s):
            return ring4[:, s, :] if s < MIX_SLOTS else ring45[:, s - MIX_SLOTS, :]

        def slot3(s, k):
            return slot_ap(s).rearrange("p (k n) -> p k n", k=k)

        s_cst, s_h, s_small = sem("constants_in"), sem("h_in"), sem("small_in")
        loaded = [sem(f"slot{s}_loaded") for s in range(6)]
        dve_step, act_step, pool_step = sem("dve_step"), sem("act_step"), sem("pool_step")
        counts = dict(
            layer_rows_in=128, modulation_slice_done=12, mod_rows_ready=1,
            mod_stored=64, mod1_in=80, gate1_in=32, mod2_in=80, gate2_in=32, router_in=64, gain_rows_in=48,
            projection_done=28, projection_evacuated=28, softplus_ready=2, key_exponent_ready=2, bound_gap_ready=0,
            bound_log_ready=0, decay_scanned=2, key_ready=2, level_gap=2 * LEVELS, level_exp=2 * LEVELS,
            level_ready=1 + 2 * LEVELS, level_scored=1 + 2 * LEVELS, level_kept=1 + 2 * LEVELS, state_gap=2,
            state_exp=2, state_operands_ready=4, keys_turned=6, keys_copied=6, state_summed=6, state_kept=6,
            head_gate_ready=1, mix_done=NT, mix_squares=1, mix_mean=1, mix_root=1, mix_ready=NT, mix_turned=NT,
            mix_copied=NT, qk_mean=1, qk_root=1, qk_inverse_ready=1, qk_ready=1, qk_turned=2 + 2 * NT,
            qk_copied=2 + 2 * NT, scores_done=NT * B_HEADS, scores_max=NT * B_HEADS, probs_ready=NT * B_HEADS,
            probs_turned=NT * B_HEADS, probs_copied=NT * B_HEADS, attended=NT * B_HEADS, attn_ready=NT,
            attn_turned=NT, attn_copied=NT, merge_gate_done=2 * KD, merge_sigmoid=2 * KD, branch_done=2 * KD,
            merged=2 * KD, residual_done=2 * NT, residual_added=2 * NT, moe_input_stored0=8 * NT, moe_input_stored1=8 * NT, logits_done=1,
            route_pre=1, route_exp=1, choices_ready=1, ranks_done=1, table_operands_ready=1, table_done=1,
            routed=1, y_gathered0=16 * NT, y_gathered1=16 * NT, y_used=NT)
        signal = {n: Signal(sem(n), k) for n, k in counts.items()}
        layer_rows_in, modulation_slice_done = signal["layer_rows_in"], signal["modulation_slice_done"]
        mod_rows_ready, mod_stored, mod1_in, gate1_in = (signal[n] for n in (
            "mod_rows_ready", "mod_stored", "mod1_in", "gate1_in"))
        mod2_in, gate2_in, router_in, gain_rows_in = (signal[n] for n in (
            "mod2_in", "gate2_in", "router_in", "gain_rows_in"))
        projection_done, projection_evacuated, softplus_ready, key_exponent_ready = (signal[n] for n in (
            "projection_done", "projection_evacuated", "softplus_ready", "key_exponent_ready"))
        bound_gap_ready, bound_log_ready, decay_scanned, key_ready = (signal[n] for n in (
            "bound_gap_ready", "bound_log_ready", "decay_scanned", "key_ready"))
        level_gap, level_exp, level_ready, level_scored = (signal[n] for n in (
            "level_gap", "level_exp", "level_ready", "level_scored"))
        level_kept, state_gap, state_exp, state_operands_ready = (signal[n] for n in (
            "level_kept", "state_gap", "state_exp", "state_operands_ready"))
        keys_turned, keys_copied, state_summed, state_kept = (signal[n] for n in (
            "keys_turned", "keys_copied", "state_summed", "state_kept"))
        head_gate_ready, mix_done, mix_squares, mix_mean = (signal[n] for n in (
            "head_gate_ready", "mix_done", "mix_squares", "mix_mean"))
        mix_root, mix_ready, mix_turned, mix_copied = (signal[n] for n in (
            "mix_root", "mix_ready", "mix_turned", "mix_copied"))
        qk_mean, qk_root, qk_inverse_ready, qk_ready = (signal[n] for n in (
            "qk_mean", "qk_root", "qk_inverse_ready", "qk_ready"))
        qk_turned, qk_copied, scores_done, scores_max = (signal[n] for n in (
            "qk_turned", "qk_copied", "scores_done", "scores_max"))
        probs_ready, probs_turned, probs_copied, attended = (signal[n] for n in (
            "probs_ready", "probs_turned", "probs_copied", "attended"))
        attn_ready, attn_turned, attn_copied, merge_gate_done = (signal[n] for n in (
            "attn_ready", "attn_turned", "attn_copied", "merge_gate_done"))
        merge_sigmoid, branch_done, merged, residual_done = (signal[n] for n in (
            "merge_sigmoid", "branch_done", "merged", "residual_done"))
        residual_added, logits_done, route_pre = (signal[n] for n in (
            "residual_added", "logits_done", "route_pre"))
        route_exp, choices_ready, ranks_done, table_operands_ready = (signal[n] for n in (
            "route_exp", "choices_ready", "ranks_done", "table_operands_ready"))
        table_done, routed, y_used = (signal[n] for n in (
            "table_done", "routed", "y_used"))
        moe_input_stored = [signal["moe_input_stored0"], signal["moe_input_stored1"]]
        y_gathered = [signal["y_gathered0"], signal["y_gathered1"]]
        fin_in = sem("final_gain_in")
        cact_ready, lb_ready = sem("conditioning_ready"), sem("bounds_ready")
        lb_exp, lb_pre = sem("bounds_exp"), sem("bounds_pre")
        y_clear, y_cleared = sem("zeros_ready"), sem("outputs_cleared")
        xg_clear = sem("gather_buffers_cleared")
        norm_tiles = [NT, NT, NT, NT - LAT0, NT - LAT0]
        norm_sems = {n: sem(f"norm_{n}") for n in ("squares", "mean", "root", "ready", "turned", "copied")}
        nrm = [Family(norm_sems, {n: i for n in ("squares", "mean", "root")} |
                      {n: sum(norm_tiles[:i]) for n in ("ready", "turned", "copied")}) for i in range(2 * DEPTH + 1)]
        moe_names = ["idx_ready", "xg_in0", "xg_in1", "xg_turned", "xgT_ready", "up_done", "silu_ready",
                     "h_ready", "h_turned", "hT_ready", "down_done", "y_copied", "y_stored0", "y_stored1"]
        first_counts = {n: {"xg_in": 16 * PAIRS, "y_stored": 32 * PAIRS}.get(n[:-1], NE) for n in moe_names}
        main_sems = {n: sem(f"expert_{n}") for n in moe_names}
        main = [Family(main_sems, {n: L * first_counts[n] for n in moe_names}) for L in range(DEPTH)]
        over_names = [n for n in moe_names if n[-1] != "1"] + ["loaded"]
        over = [Family({n: sem(f"over_{n}_{L}") for n in over_names}, {n: 0 for n in over_names})
                for L in range(DEPTH)]
        out_done = sem("out_stored")
        passed = sem("waits_passed")

        mod_rows = mod_dram

        def tiles_of(L):
            return list(range(NT)) if L < DEPTH - 1 else list(range(LAT0, NT))

        def stream(tile):
            return 0 if tile < LAT0 else 1

        def tk(tile):
            return slice(tile * P, (tile + 1) * P)

        def sections(L):
            return [("gz", tiles_of(L)), ("bq", tiles_of(L)), ("bkv", list(range(NT)))]

        def release(L, name):
            nt = len(tiles_of(L))
            ends = {"ff": 4, "fb": 8, "q": 12, "i": 12 + NT}
            ends["gz"] = ends["i"] + nt
            ends["bq"] = ends["gz"] + nt
            ends["bkv"] = ends["bq"] + NT
            if name.startswith("ada"):
                return modulation_slice_done.at(L, int(name[3:]) + 1)
            if name in ends:
                return projection_done.at(L, ends[name])
            z = {"z8_0": 4, "z8_1": 8, "z9_0": 12, "z9_1": 16}
            if name in z:
                return merge_gate_done.at(L, z[name])
            if name in ("up_a", "up_b"):
                return branch_done.at(L, 8 if name == "up_a" else 16)
            return residual_done.at(L, nt if name == "out0" else 2 * nt)

        def schedule(L):
            units = [("unit", n, t) for n, ts in sections(L) for t in ts]
            steps = [("step", j) for j in range(1 + 2 * LEVELS)]
            sched = []
            while units or steps:
                if units:
                    sched.append(units.pop(0))
                if steps:
                    sched.append(steps.pop(0))
            return sched

        UPDATES = [(0, 0), (1, 1), (0, 1), (1, 0), (0, 2), (1, 3)]
        BEFORE = {(0, 0): None, (1, 1): None, (0, 1): 0, (1, 0): 1, (0, 2): 2, (1, 3): 3}
        ENTER = [{1: 0, 2: 2, 3: 4}, {0: 1, 3: 3, 2: 5}]

        block = ctx.enter_context(nc.Block())

        def alone(eng):
            eng.sem_inc(passed)

        @block.sync
        def _(sp):
            sp.dma_start(cst[:], consts).then_inc(s_cst, 16)
            sp.dma_start(masks_in, masks).then_inc(s_cst, 16)
            sp.dma_start(cin[:, :, 0], c_ctx.rearrange("(k p) -> p k", p=P), allow_slow_non_contiguous=True).then_inc(s_small, 16)
            sp.dma_start(cin[:, :, 1], c.rearrange("o (k p) -> p (o k)", p=P), allow_slow_non_contiguous=True).then_inc(s_small, 16)
            for l_ in range(DEPTH):
                for d in range(2):
                    sp.dma_start(lbt[:, l_, d * HEADS:(d + 1) * HEADS], lb_logits[d, l_].rearrange("(h p) -> p h", p=P),
                                 allow_slow_non_contiguous=True).then_inc(s_small, 16)
            for t in range(NT):
                src = ctx_in[0, tk(t), :] if t < LAT0 else x[0, (t - LAT0) * P:(t - LAT0 + 1) * P, :]
                sp.dma_start(h[:, t, :], src).then_inc(s_h, 16)

            def w_source(L, name):
                if name.startswith("ada"):
                    n = int(name[3:])
                    return w_ada[L][:, n * 512:(n + 1) * 512].rearrange("(k p) n -> p k n", p=P), KD
                cols = {"q": (Q0, AW), "ff": (FF0, AW), "fb": (FB0, AW), "i": (I0, AW), "gz": (GZ0, AW), "bq": (BQ0, AW),
                        "bkv": (BKV0, Z80 - BKV0), "z8_0": (Z80, 512), "z8_1": (Z80 + 512, 512), "z9_0": (Z90, 512),
                        "z9_1": (Z90 + 512, 512)}
                if name in cols:
                    a, n = cols[name]
                    return w_in[L][:, a:a + n].rearrange("(k p) n -> p k n", p=P), KD
                if name in ("up_a", "up_b"):
                    return (w_up_a if name == "up_a" else w_up_b)[L].rearrange("(k p) n -> p k n", p=P), 4
                n = int(name[3:])
                return w_out[L][:, n * 512:(n + 1) * 512].rearrange("(k p) n -> p k n", p=P), KD

            for L in range(DEPTH):
                for name, (slot, use, last) in where[L].items():
                    if last:
                        sp.wait_ge(*release(L, last))
                    elif L:
                        sp.wait_ge(*main[L - 1].at("up_done", NE if slot >= 2 else NE - 1))
                    src, k = w_source(L, name)
                    n = src.shape[-1]
                    dst = slot_ap(slot)[:, 0:k * n].rearrange("p (k n) -> p k n", k=k)
                    sp.dma_start(dst, src).then_inc(loaded[slot], 16)

                experts = [w_gate[L].rearrange("e (k p) n -> p e k n", p=P), w_up[L].rearrange("e (k p) n -> p e k n", p=P),
                           w_down[L].rearrange("e (k p) n -> p e k n", p=P)]
                done = ("up_done", "up_done", "down_done")

                def fetch_pair(i, first):
                    for par in range(2):
                        for j in range(3):
                            s = EXPERT_SLOTS[par][j]
                            e = 2 * i + par
                            if first:
                                if s < MIX_SLOTS:
                                    sp.wait_ge(*release(L, tenant[L][s]))
                                else:
                                    sp.wait_ge(*attn_turned.at(L, len(tiles_of(L))))
                                src = experts[j][:, e]
                            else:
                                src = experts[j][:, bass.ds(e, 1)].rearrange("p o k n -> p (o k) n")
                                sp.wait_ge(*main[L].at(done[j], e - 1))
                                alone(sp)
                            sp.dma_start(slot3(s, KD if j < 2 else 4), src).then_inc(loaded[s], 16)

                fetch_pair(0, True)
                with sp.Fori(1, PAIRS) as i:
                    fetch_pair(i, False)
                sp.wait_ge(*routed.at(L, 1))
                n_over = sp.value_load(numi[0:1, OVER:OVER + 1], min_val=0, max_val=OVER)
                with sp.If(n_over > 0):
                    sp.wait_ge(*main[L].at("down_done", NE))
                    with sp.Fori(0, n_over) as j:
                        e = sp.value_load(numi[0:1, bass.ds(j, 1)], min_val=0, max_val=NE - 1)
                        for m in range(3):
                            sp.dma_start(slot3(EXPERT_SLOTS[0][m], KD if m < 2 else 4),
                                         experts[m][:, bass.ds(e, 1)].rearrange("p o k n -> p (o k) n")
                                         ).then_inc(over[L].sem("loaded"), 16)
                        sp.wait_ge(*over[L].at("down_done", j + 1))
                        alone(sp)

            sp.wait_ge(out_done, 16 * (NT - LAT0))

        @block.tensor
        def _(pe):
            pe.wait_ge(s_cst, 32)

            def mm(o, a, b, first, last):
                return pe.matmul(o, a, b, start=first, stop=last)

            def turn_norm(L, which, tiles):
                s = nrm[2 * L + which]
                for i, t in enumerate(tiles):
                    pe.wait_ge(*s.at("ready", i + 1))
                    if i >= 2:
                        pe.wait_ge(*s.at("copied", i - 1))
                    for k in range(KD):
                        ins = pe.transpose(ps[:, 2 * (i % 2) + k // 4, (k % 4) * P:(k % 4 + 1) * P],
                                           xn[which][:, i % 2, tk(k)], ident)
                    ins.then_inc(s.sem("turned"), 1)

            for L in range(DEPTH):
                tiles = tiles_of(L)
                q0 = tiles[0] * P
                nq = len(tiles) * P
                nt = len(tiles)

                def take(name):
                    slot, use, _ = where[L][name]
                    pe.wait_ge(loaded[slot], 16 * (use + 1))
                    return slot

                pe.wait_ge(cact_ready, 1)
                for n in range(12):
                    w = slot3(take(f"ada{n}"), KD)
                    for k in range(KD):
                        for m in range(4):
                            ins = mm(ps[32 * m:32 * m + 2, 5 + n // 4, tk(n % 4)], cact[:, k, :], w[:, k, tk(m)],
                                     k == 0, k == KD - 1)
                    ins.then_inc(modulation_slice_done.sem, 1)

                turn_norm(L, 0, range(NT))

                g = 0
                pe.wait_ge(*nrm[2 * L].at("copied", NT))
                for name in ("ff", "fb", "q"):
                    w = slot3(take(name), KD)
                    a = 0 if name != "q" else q0
                    for m in range(HEADS):
                        if g >= 4:
                            pe.wait_ge(*projection_evacuated.at(L, g - 3))
                        for k in range(KD):
                            ins = mm(ps[:, 4 + g % 4, 0:TOKENS - a], w[:, k, tk(m)], xT[:, k, a:TOKENS], k == 0, k == KD - 1)
                        ins.then_inc(projection_done.sem, 1)
                        g += 1

                def natural_unit(name, t):
                    nonlocal g
                    slot, use, _ = where[L][name]
                    n = 512 if name != "bkv" else Z80 - BKV0
                    pe.wait_ge(loaded[slot], 16 * (use + 1))
                    w = slot_ap(slot)[:, 0:KD * n].rearrange("p (k n) -> p k n", k=KD)
                    pe.wait_ge(*projection_evacuated.at(L, g - 3))
                    for k in range(KD):
                        ins = mm(ps[:, 4 + g % 4, 0:n], xT[:, k, tk(t)], w[:, k, :], k == 0, k == KD - 1)
                    ins.then_inc(projection_done.sem, 1)
                    g += 1

                for t in range(NT):
                    natural_unit("i", t)

                def level_scores(j):
                    pe.wait_ge(*level_ready.at(L, j + 1))
                    if j:
                        pe.wait_ge(*level_kept.at(L, j))
                    w = wlv[j % 2]
                    for t in tiles:
                        for hd in range(HEADS):
                            ins = mm(ps[:, t, tk(hd)], w[:, hd, tk(t)], (w if j else qf)[:, hd, tk(t)], True, True)
                    ins.then_inc(level_scored.sem, 1)

                for what in schedule(L):
                    if what[0] == "unit":
                        natural_unit(what[1], what[2])
                    else:
                        level_scores(what[1])

                for u, (d, t) in enumerate(UPDATES):
                    if u == 0:
                        pe.wait_ge(*state_operands_ready.at(L, 2))
                        pe.wait_ge(*projection_evacuated.at(L, g))
                    if u >= 2:
                        pe.wait_ge(*keys_copied.at(L, u - 1))
                    for hd in range(HEADS):
                        ins = pe.transpose(ps[:, 4 + u % 2, tk(hd)], kg[d][:, hd, tk(t)], ident)
                    ins.then_inc(keys_turned.sem, 1)
                    pe.wait_ge(*keys_copied.at(L, u + 1))
                    if u >= 2:
                        pe.wait_ge(*state_kept.at(L, u - 1))
                    for hd in range(HEADS):
                        ins = mm(ps[:, 6 + u % 2, tk(hd)], kdn[:, u % 2, tk(hd)], v[:, t, tk(hd)], True, True)
                    ins.then_inc(state_summed.sem, 1)

                pe.wait_ge(*state_kept.at(L, len(UPDATES)))
                pe.wait_ge(*state_operands_ready.at(L, 4))
                pe.wait_ge(*level_kept.at(L, 1 + 2 * LEVELS))
                for t in tiles:
                    for hd in range(HEADS):
                        parts = [(amat[:, t, hd, :], v[:, t, tk(hd)])]
                        for d in range(2):
                            if t in ENTER[d]:
                                parts.append((cum[d][:, hd, tk(t)], states[:, ENTER[d][t], hd, :]))
                        for n, (a, b) in enumerate(parts):
                            ins = mm(ps[:, t, tk(hd)], a, b, n == 0, n == len(parts) - 1)
                    ins.then_inc(mix_done.sem, 1)

                pe.wait_ge(*qk_ready.at(L, 1))
                turned = 0
                for kv in range(B_KV):
                    for t in range(NT):
                        ins = pe.transpose(ps[0:HD, 4 + turned % 2, tk(t)], bkv[:, t, kv * HD:(kv + 1) * HD], ident)
                    ins.then_inc(qk_turned.sem, 1)
                    turned += 1
                for t in tiles:
                    for half in range(2):
                        pe.wait_ge(*qk_copied.at(L, turned - 1))
                        for m in range(4):
                            hd = 4 * half + m
                            ins = pe.transpose(ps[0:HD, 4 + turned % 2, tk(m)], bq[:, t, hd * HD:(hd + 1) * HD], ident)
                        ins.then_inc(qk_turned.sem, 1)
                        turned += 1

                steps = [(t, hd) for t in tiles for hd in range(B_HEADS)]
                keys = [(LAT0 if t < LAT0 else NT) for t, _ in steps]
                pe.wait_ge(*qk_copied.at(L, turned))
                for i in range(len(steps) + 2):
                    if i < len(steps):
                        t, hd = steps[i]
                        if i >= 2:
                            pe.wait_ge(*probs_ready.at(L, i - 1))
                        mm(ps[:, 4 + i % 2, 0:keys[i] * P], qT[0:HD, hd, tk(t)], kT[0:HD, hd // GROUP, 0:keys[i] * P],
                           True, True).then_inc(scores_done.sem, 1)
                    if 1 <= i <= len(steps):
                        n = i - 1
                        pe.wait_ge(*probs_ready.at(L, n + 1))
                        if n >= 2:
                            pe.wait_ge(*probs_copied.at(L, n - 1))
                        for kc in range(keys[n]):
                            ins = pe.transpose(ps[:, 6 + n % 2, tk(kc)], probs[:, n % 2, tk(kc)], ident)
                        ins.then_inc(probs_turned.sem, 1)
                    if i >= 2:
                        n = i - 2
                        t, hd = steps[n]
                        pe.wait_ge(*probs_copied.at(L, n + 1))
                        if hd == 0:
                            pe.wait_ge(*mix_ready.at(L, nt))
                            if n >= 2 * B_HEADS:
                                pe.wait_ge(*attn_ready.at(L, n // B_HEADS - 1))
                        for kc in range(keys[n]):
                            ins = mm(ps[:, (n // B_HEADS) % 2, hd * HD:(hd + 1) * HD], probsT[:, n % 2, tk(kc)],
                                     bkv[:, kc, (B_KV + hd // GROUP) * HD:(B_KV + hd // GROUP + 1) * HD],
                                     kc == 0, kc == keys[n] - 1)
                        ins.then_inc(attended.sem, 1)

                for i, t in enumerate(tiles):
                    if i >= 2:
                        pe.wait_ge(*mix_copied.at(L, i - 1))
                    for k in range(4):
                        ins = pe.transpose(ps[:, 2 + i % 2, tk(k)], gz[:, t, tk(k)], ident)
                    ins.then_inc(mix_turned.sem, 1)
                for i, t in enumerate(tiles):
                    pe.wait_ge(*attn_ready.at(L, i + 1))
                    if i >= 2:
                        pe.wait_ge(*attn_copied.at(L, i - 1))
                    for k in range(4):
                        ins = pe.transpose(ps[:, 4 + i % 2, tk(k)], bq[:, t, tk(k)], ident)
                    ins.then_inc(attn_turned.sem, 1)

                pe.wait_ge(*mix_copied.at(L, nt))
                pe.wait_ge(*attn_copied.at(L, nt))
                for ph, (zs, up, br) in enumerate(((("z8_0", "z8_1"), "up_a", aT), (("z9_0", "z9_1"), "up_b", bT))):
                    for m in range(KD):
                        n = ph * KD + m
                        w = slot3(take(zs[m // 4]), KD)
                        if n >= 2:
                            pe.wait_ge(*merge_sigmoid.at(L, n - 1))
                        for k in range(KD):
                            ins = mm(ps[:, 4 + n % 2, 0:nq], w[:, k, tk(m % 4)], xT[:, k, q0:TOKENS], k == 0, k == KD - 1)
                        ins.then_inc(merge_gate_done.sem, 1)
                        w = slot3(take(up), 4)
                        if n >= 2:
                            pe.wait_ge(*merged.at(L, n - 1))
                        for k in range(4):
                            ins = mm(ps[:, 6 + n % 2, 0:nq], w[:, k, tk(m)], br[:, k, q0:TOKENS], k == 0, k == 3)
                        ins.then_inc(branch_done.sem, 1)

                pe.wait_ge(*merged.at(L, 2 * KD))
                n = 0
                for half in range(2):
                    w = slot3(take(f"out{half}"), KD)
                    for t in tiles:
                        if n >= 4:
                            pe.wait_ge(*residual_added.at(L, n - 3))
                        for k in range(KD):
                            ins = mm(ps[:, n % 4, :], mT[:, k, tk(t)], w[:, k, :], k == 0, k == KD - 1)
                        ins.then_inc(residual_done.sem, 1)
                        n += 1

                pe.wait_ge(*residual_added.at(L, n))
                turn_norm(L, 1, tiles)
                pe.wait_ge(*nrm[2 * L + 1].at("copied", nt))
                pe.wait_ge(*router_in.at(L, 64))
                for i, t in enumerate(tiles):
                    for k in range(KD):
                        ins = mm(ps[:, 4, i * 36:(i + 1) * 36], xT[:, k, tk(t)], wr[:, k, :], k == 0, k == KD - 1)
                ins.then_inc(logits_done.sem, 1)
                pe.wait_ge(*choices_ready.at(L, 1))
                for i in range(nt):
                    for j in range(i):
                        mm(ps[:, 5, i * NE:(i + 1) * NE], ones, both[:, j, :], j == 0, False)
                    mm(ps[:, 5, i * NE:(i + 1) * NE], cst[:, C_UP:C_UP + P], both[:, i, :], i == 0, True)
                for j in range(nt):
                    ins = mm(ps[:, 5, nt * NE:(nt + 1) * NE], ones, both[:, j, :], j == 0, j == nt - 1)
                ins.then_inc(ranks_done.sem, 1)
                pe.wait_ge(*table_operands_ready.at(L, 1))
                for j in range(2 * nt):
                    ins = mm(ps[0:CAP, 6, 0:NB], ohrow[:, j, :], ohblk[:, j, :], j == 0, j == 2 * nt - 1)
                ins.then_inc(table_done.sem, 1)

                def expert(X, b, i, par, first, weights_in):
                    pe.wait_ge(*X.at(f"xg_in{par}", 16 * (i + 1)))
                    if not first:
                        pe.wait_ge(*X.at("xgT_ready", b))
                    alone(pe)
                    for k in range(KD):
                        ins = pe.transpose(ps[:, 0, k * CAP:(k + 1) * CAP], xg[0:CAP, par, tk(k)], ident[0:CAP, 0:CAP])
                    ins.then_inc(X.sem("xg_turned"), 1)
                    pe.wait_ge(*X.at("xgT_ready", b + 1))
                    g_, u_, d_ = EXPERT_SLOTS[par]
                    weights_in(g_, i)
                    weights_in(u_, i)
                    w = ring4[:, g_:g_ + 2, :].rearrange("p s (k n) -> p s k n", k=KD)
                    for k in range(KD):
                        for hf in range(2):
                            ins = mm(ps[CAP * hf:CAP * (hf + 1), 1 + par, :].rearrange("p (s n) -> p s n", s=2),
                                     xgT[:, par, k, :], w[:, :, k, DE // 2 * hf:DE // 2 * (hf + 1)], k == 0, k == KD - 1)
                    ins.then_inc(X.sem("up_done"), 1)
                    pe.wait_ge(*X.at("h_ready", b + 1))
                    for j in range(2):
                        ins = pe.transpose(ps[:, 3, tk(j)], hid[:, par, tk(j)], ident)
                    ins.then_inc(X.sem("h_turned"), 1)
                    pe.wait_ge(*X.at("hT_ready", b + 1))
                    weights_in(d_, i)
                    if not first:
                        pe.wait_ge(*X.at("y_copied", b))
                    w = slot3(d_, 4)
                    for k in range(4):
                        for hf in range(2):
                            ins = mm(ps[CAP * hf:CAP * (hf + 1), 4, :], hT[:, par, k % 2, CAP * (k // 2):CAP * (k // 2 + 1)],
                                     w[:, k, 512 * hf:512 * (hf + 1)], k == 0, k == 3)
                    ins.then_inc(X.sem("down_done"), 1)

                def ring_in(s, i):
                    pe.wait_ge(loaded[s], 16 * (expert_use[L][s] + 1) + 16 * i)

                for par in range(2):
                    expert(main[L], par, 0, par, par == 0, ring_in)
                with pe.Fori(1, PAIRS) as i:
                    for par in range(2):
                        expert(main[L], 2 * i + par, i, par, False, ring_in)
                pe.wait_ge(*routed.at(L, 1))
                n_over = pe.value_load(numi[0:1, OVER:OVER + 1], min_val=0, max_val=OVER)
                with pe.If(n_over > 0):
                    pe.wait_ge(*main[L].at("y_copied", NE))
                    with pe.Fori(0, n_over) as j:
                        expert(over[L], j, j, 0, True, lambda s, i: pe.wait_ge(*over[L].at("loaded", 48 * j + 48)))

        @block.scalar
        def _(act):
            counted = [0]

            def link(ins):
                counted[0] += 1
                ins.then_inc(act_step, 1)
                act.wait_ge(act_step, counted[0])

            act.wait_ge(s_small, 96)
            act.activation(cact[:], cin[:], ACT.Silu).then_inc(cact_ready, 1)
            act.wait_ge(lb_pre, 1)
            act.activation(lbt[:, 5:7, :], lbt[:, 3:5, :], ACT.Exp).then_inc(lb_exp, 1)
            act.wait_ge(lb_pre, 2)
            act.activation(lbt[:, 5:7, :], lbt[:, 3:5, :], ACT.Ln).then_inc(lb_exp, 1)

            def norm(n, tiles, ready):
                s = nrm[n]
                for i, t in enumerate(tiles):
                    ready(i)
                    link(act.activation(xn[1][:, 1, :] if n % 2 else junk, h[:, t, :], ACT.Square, accum_out=stat[:, n, 0, t:t + 1]))
                link(act.copy(stat[:, n, 2, 0:1], stat[:, n, 0, tiles[0]:tiles[0] + 1]))
                act.copy(stat[:, n, 2, 0:1], stat[:, n, 0, tiles[0]:tiles[0] + 1]).then_inc(s.sem("squares"), 1)
                act.wait_ge(*s.at("mean", 1))
                act.activation(stat[:, n, 2, :], stat[:, n, 1, :], ACT.Sqrt).then_inc(s.sem("root"), 1)

            def copy_turned(n, tiles):
                s = nrm[n]
                for i, t in enumerate(tiles):
                    act.wait_ge(*s.at("turned", i + 1))
                    b = 2 * (i % 2)
                    act.copy(xT[:, :, tk(t)], ps[:, b:b + 2, :].rearrange("p b (k n) -> p (b k) n", k=4)).then_inc(s.sem("copied"), 1)

            for L in range(DEPTH):
                tiles = tiles_of(L)
                q0 = tiles[0] * P
                nq = len(tiles) * P
                nt = len(tiles)
                if L == 0:
                    norm(0, range(NT), lambda i: act.wait_ge(s_h, 16 * NT))
                else:
                    norm(2 * L, range(NT), lambda i: act.wait_ge(*y_used.at(L - 1, 4)))
                copy_turned(2 * L, range(NT))

                g = 0
                for d in range(2):
                    for m in range(HEADS):
                        act.wait_ge(*projection_done.at(L, g + 1))
                        if d and m == 0:
                            act.wait_ge(*decay_scanned.at(L, 1))
                        act.copy(wlv[0][:, m, :], ps[:, 4 + g % 4, :])
                        act.activation(wlv[1][:, m, :], ps[:, 4 + g % 4, :], ACT.Abs).then_inc(projection_evacuated.sem, 1)
                        g += 1
                    act.wait_ge(*projection_evacuated.at(L, g))
                    link(act.activation(wlv[1], wlv[1], ACT.Exp, scale=-1.0))
                    act.activation(wlv[1], wlv[1], ACT.Ln, bias=1.0).then_inc(softplus_ready.sem, 1)
                    act.wait_ge(*key_exponent_ready.at(L, d + 1))
                    for m in range(HEADS):
                        ins = act.activation(kg[d][:, m, :], kg[d][:, m, :], ACT.Exp,
                                             bias=lbac[:, 1, d * HEADS + m:d * HEADS + m + 1] if L else 0.0)
                    ins.then_inc(key_ready.sem, 1)
                    if L:
                        act.wait_ge(*bound_gap_ready.at(L, d + 1))
                        link(act.activation(wlv[0], wlv[0], ACT.Abs))
                        link(act.activation(wlv[0], wlv[0], ACT.Exp, scale=-1.0))
                        act.activation(wlv[0], wlv[0], ACT.Ln, bias=1.0).then_inc(bound_log_ready.sem, 1)
                for m in range(HEADS):
                    act.wait_ge(*projection_done.at(L, g + 1))
                    act.activation(qf[:, m, q0:TOKENS], ps[:, 4 + g % 4, 0:nq], ACT.Silu).then_inc(projection_evacuated.sem, 1)
                    g += 1

                def unit(name, t):
                    nonlocal g
                    n = 512 if name != "bkv" else Z80 - BKV0
                    act.wait_ge(*projection_done.at(L, g + 1))
                    dst = {"i": v, "gz": gz, "bq": bq, "bkv": bkv}[name]
                    act.copy(dst[:, t, :], ps[:, 4 + g % 4, 0:n]).then_inc(projection_evacuated.sem, 1)
                    g += 1

                for t in range(NT):
                    unit("i", t)
                for what in schedule(L):
                    if what[0] == "unit":
                        unit(what[1], what[2])
                    elif what[1] < 2 * LEVELS:
                        j = what[1] + 1
                        act.wait_ge(*level_gap.at(L, j))
                        w = wlv[j % 2][:, :, q0:TOKENS]
                        act.activation(w, w, ACT.Exp).then_inc(level_exp.sem, 1)

                for d in range(2):
                    act.wait_ge(*state_gap.at(L, d + 1))
                    act.activation(wlv[d], wlv[d], ACT.Exp)
                    last = cum[d].rearrange("p h (t n) -> p (h t) n", n=P)[:, :, P - 1 if d == 0 else 0]
                    link(act.activation(eb[:, d, :], last, ACT.Exp))
                    w = cum[d][:, :, q0:TOKENS]
                    act.activation(w, w, ACT.Exp).then_inc(state_exp.sem, 1)
                for u in range(len(UPDATES)):
                    act.wait_ge(*keys_turned.at(L, u + 1))
                    if u >= 2:
                        act.wait_ge(*state_summed.at(L, u - 1))
                    act.copy(kdn[:, u % 2, :], ps[:, 4 + u % 2, :]).then_inc(keys_copied.sem, 1)
                act.wait_ge(*projection_evacuated.at(L, g))
                w = gz[:, tiles[0]:NT, :]
                act.activation(w, w, ACT.Silu).then_inc(head_gate_ready.sem, 1)
                for i, t in enumerate(tiles):
                    act.wait_ge(*mix_done.at(L, i + 1))
                    for hd in range(HEADS):
                        n = 4 * t + hd
                        link(act.activation(junk[:, (n % 8) * P:(n % 8 + 1) * P], ps[:, t, tk(hd)], ACT.Square,
                                            accum_out=hst[:, 0, n:n + 1]))
                act.copy(hst[:, 2, 0:1], hst[:, 0, 4 * tiles[0]:4 * tiles[0] + 1]).then_inc(mix_squares.sem, 1)
                act.wait_ge(*mix_mean.at(L, 1))
                act.activation(hst[:, 2, :], hst[:, 1, :], ACT.Sqrt).then_inc(mix_root.sem, 1)
                act.wait_ge(*qk_mean.at(L, 1))
                act.activation(qst[:, 2, :], qst[:, 1, :], ACT.Sqrt).then_inc(qk_root.sem, 1)

                turned = 0
                for kv in range(B_KV):
                    act.wait_ge(*qk_turned.at(L, turned + 1))
                    act.copy(kT[0:HD, kv, :], ps[0:HD, 4 + turned % 2, :]).then_inc(qk_copied.sem, 1)
                    turned += 1
                for t in tiles:
                    for half in range(2):
                        act.wait_ge(*qk_turned.at(L, turned + 1))
                        act.copy(qT[0:HD, 4 * half:4 * half + 4, tk(t)],
                                 ps[0:HD, 4 + turned % 2, :].rearrange("p (m n) -> p m n", m=4)).then_inc(qk_copied.sem, 1)
                        turned += 1
                for i in range(nt * B_HEADS):
                    t = tiles[i // B_HEADS]
                    nk = (LAT0 if t < LAT0 else NT) * P
                    act.wait_ge(*scores_max.at(L, i + 1))
                    if i >= 2:
                        act.wait_ge(*probs_turned.at(L, i - 1))
                    act.activation(probs[:, i % 2, 0:nk], ps[:, 4 + i % 2, 0:nk], ACT.Exp, bias=mxs[:, 1, i:i + 1],
                                   scale=HD ** -0.5, accum_out=mxs[:, 2, i:i + 1]).then_inc(probs_ready.sem, 1)
                for i, t in enumerate(tiles):
                    act.wait_ge(*mix_turned.at(L, i + 1))
                    act.copy(aT[:, :, tk(t)], ps[:, 2 + i % 2, :].rearrange("p (k n) -> p k n", k=4)).then_inc(mix_copied.sem, 1)
                for i, t in enumerate(tiles):
                    act.wait_ge(*attn_turned.at(L, i + 1))
                    act.copy(bT[:, :, tk(t)], ps[:, 4 + i % 2, :].rearrange("p (k n) -> p k n", k=4)).then_inc(attn_copied.sem, 1)

                for n in range(2 * KD):
                    act.wait_ge(*merge_gate_done.at(L, n + 1))
                    if n >= 2:
                        act.wait_ge(*merged.at(L, n - 1))
                    act.activation(sgm[:, n % 2, 0:nq], ps[:, 4 + n % 2, 0:nq], ACT.Sigmoid).then_inc(merge_sigmoid.sem, 1)

                norm(2 * L + 1, tiles, lambda i: act.wait_ge(*residual_added.at(L, nt + i + 1)))
                copy_turned(2 * L + 1, tiles)
                act.wait_ge(*route_pre.at(L, 1))
                act.activation(grp[:, 2, 0:nt, :], grp[:, 1, 0:nt, :], ACT.Exp)
                act.activation(one[:, 5, 0:nt], one[:, 4, 0:nt], ACT.Exp).then_inc(route_exp.sem, 1)

                def expert(X, b, i, par, early, column):
                    act.wait_ge(*X.at("up_done", b + 1))
                    if early >= 2:
                        act.wait_ge(*X.at("h_ready", b - 1))
                    act.activation(sg[:, par, :], ps[:, 1 + par, 0:DE // 2], ACT.Silu).then_inc(X.sem("silu_ready"), 1)
                    act.wait_ge(*X.at("down_done", b + 1))
                    if early >= 2:
                        act.wait_ge(*X.at(f"y_stored{par}", 32 * i))
                    act.copy(yb[:, par, :], ps[:, 4, :]).then_inc(X.sem("y_copied"), 1)
                    act.wait_ge(*X.at("y_copied", b + 1))
                    for hf in range(2):
                        dst = y_dram[:, column, 512 * hf:512 * (hf + 1)]
                        if isinstance(column, bass.DynSlice):
                            dst = dst.rearrange("c o n -> c (o n)")
                        act.dma_start(dst, yb[CAP * hf:CAP * (hf + 1), par, :]).then_inc(X.sem(f"y_stored{par}"), 16)

                for par in range(2):
                    expert(main[L], par, 0, par, par, par)
                with act.Fori(1, PAIRS) as i:
                    for par in range(2):
                        expert(main[L], 2 * i + par, i, par, 2, bass.ds(2 * i + par, 1))
                act.wait_ge(*routed.at(L, 1))
                n_over = act.value_load(numi[0:1, OVER:OVER + 1], min_val=0, max_val=OVER)
                with act.If(n_over > 0):
                    act.wait_ge(*main[L].at("y_stored0", 32 * PAIRS))
                    act.wait_ge(*main[L].at("y_stored1", 32 * PAIRS))
                    with act.Fori(0, n_over) as j:
                        expert(over[L], j, j, 0, 0, bass.ds(j + NE, 1))

            norm(2 * DEPTH, range(LAT0, NT), lambda i: act.wait_ge(*y_used.at(DEPTH - 1, NT - LAT0)))
            for i, t in enumerate(range(LAT0, NT)):
                act.wait_ge(*nrm[2 * DEPTH].at("ready", i + 1))
                act.dma_start(out[0, (t - LAT0) * P:(t - LAT0 + 1) * P, :], xn[0][:, i, :]).then_inc(out_done, 16)

        @block.vector
        def _(dve):
            counted = [0]

            def link(ins):
                counted[0] += 1
                ins.then_inc(dve_step, 1)
                dve.wait_ge(dve_step, counted[0])

            def bc(ap, shape):
                return ap.unsqueeze(len(ap.shape)).broadcast_to(shape)

            dve.wait_ge(s_small, 96)
            dve.wait_ge(s_cst, 32)
            link(dve.tensor_copy(msk[:].rearrange("p a b n -> p (a b n)"), masks_in))
            link(dve.tensor_tensor(lbt[:, 2, :], lbt[:, 0, :], lbt[:, 1, :], ALU.max))
            dve.tensor_tensor(lbt[:, 3, :], lbt[:, 0, :], lbt[:, 2, :], ALU.subtract)
            dve.tensor_tensor(lbt[:, 4, :], lbt[:, 1, :], lbt[:, 2, :], ALU.subtract).then_inc(lb_pre, 1)
            dve.wait_ge(lb_exp, 1)
            link(dve.tensor_tensor(lbt[:, 7, :], lbt[:, 5, :], lbt[:, 6, :], ALU.add))
            link(dve.reciprocal(lbt[:, 7, :], lbt[:, 7, :]))
            link(dve.tensor_tensor(lbt[:, 8, :], lbt[:, 5, :], lbt[:, 7, :], ALU.mult))
            link(dve.tensor_tensor(lbt[:, 9, :], lbt[:, 6, :], lbt[:, 7, :], ALU.mult))
            link(dve.tensor_tensor(lbt[:, 9, :], lbt[:, 8, :], lbt[:, 9, :], ALU.add))
            link(dve.tensor_tensor(lbt[:, 9, :], lbt[:, 9, :], lbt[:, 8, :], ALU.subtract))
            link(dve.tensor_scalar(lbt[:, 2, :], lbt[:, 9, :], -1.0, 1.0, ALU.mult, ALU.add))
            dve.tensor_scalar(lbt[:, 3, :], lbt[:, 9, :], TINY, None, ALU.max)
            dve.tensor_scalar(lbt[:, 4, :], lbt[:, 2, :], TINY, None, ALU.max).then_inc(lb_pre, 1)
            link(dve.tensor_scalar(lbt[:, 0, :], lbt[:, 9, :], 0.0, -BIG, ALU.is_equal, ALU.mult))
            link(dve.tensor_scalar(lbt[:, 1, :], lbt[:, 2, :], 0.0, -BIG, ALU.is_equal, ALU.mult))
            dve.wait_ge(lb_exp, 2)
            link(dve.tensor_tensor(lbac[:, 0, :], lbt[:, 5, :], lbt[:, 0, :], ALU.add))
            dve.tensor_tensor(lbac[:, 1, :], lbt[:, 6, :], lbt[:, 1, :], ALU.add).then_inc(lb_ready, 1)

            def norm_scale(n):
                s = nrm[n]
                dve.wait_ge(*s.at("squares", 1))
                a = LAT0 if n >= 2 * DEPTH - 1 else 0
                if a:
                    link(dve.memset(stat[:, n, 1, 0:a], 1.0))
                dve.tensor_scalar(stat[:, n, 1, a:], stat[:, n, 0, a:], 1.0 / D, EPS, ALU.mult, ALU.add).then_inc(s.sem("mean"), 1)
                dve.wait_ge(*s.at("root", 1))
                link(dve.reciprocal(stat[:, n, 3, :], stat[:, n, 2, :]))

            def norm_rows(L, which, tiles, mod_in):
                n = 2 * L + which
                s = nrm[n]
                norm_scale(n)
                dve.wait_ge(*mod_in.at(L, 16 * 5))
                for st in range(stream(tiles[0]), 2):
                    link(dve.scalar_tensor_tensor(ab[which][:, st, 0, :], ab[which][:, st, 0, :], 1.0, gbc,
                                                  ALU.add, ALU.mult))
                for i, t in enumerate(tiles):
                    if i >= 2:
                        dve.wait_ge(*s.at("turned", i - 1))
                        if which:
                            dve.wait_ge(*moe_input_stored[i % 2].at(L, 16 * (i // 2)))
                    xx = xn[which][:, i % 2, :]
                    st = stream(t)
                    link(dve.scalar_tensor_tensor(xx, h[:, t, :], stat[:, n, 3, t:t + 1], ab[which][:, st, 0, :],
                                                  ALU.mult, ALU.mult))
                    dve.tensor_tensor(xx, xx, ab[which][:, st, 1, :], ALU.add).then_inc(s.sem("ready"), 1)

            for L in range(DEPTH):
                tiles = tiles_of(L)
                t0 = tiles[0]
                q0 = t0 * P
                nq = len(tiles) * P
                nt = len(tiles)
                dve.wait_ge(*layer_rows_in.at(L, 16 * 8))
                for q_ in range(3):
                    dve.wait_ge(*modulation_slice_done.at(L, 4 * q_ + 4))
                    for m in range(4):
                        r = modR[32 * m:32 * m + 2, 4 * q_:4 * q_ + 4, :]
                        ins = dve.tensor_tensor(r, ps[32 * m:32 * m + 2, 5 + q_, :].rearrange("p (n c) -> p n c", n=4),
                                                r, ALU.add)
                ins.then_inc(mod_rows_ready.sem, 1)
                norm_rows(L, 0, list(range(NT)), mod1_in)

                for d in range(2):
                    dve.wait_ge(*softplus_ready.at(L, d + 1))
                    link(dve.scalar_tensor_tensor(wlv[1], wlv[0], 0.0, wlv[1], ALU.min, ALU.subtract))
                    dve.tensor_tensor(kg[d], wlv[1], wlv[0], ALU.subtract).then_inc(key_exponent_ready.sem, 1)
                    if L:
                        if d == 0:
                            dve.wait_ge(lb_ready, 1)
                        dve.wait_ge(*key_exponent_ready.at(L, d + 1))
                        for m in range(HEADS):
                            n = d * HEADS + m
                            ins = dve.tensor_scalar(wlv[1][:, m, :], wlv[1][:, m, :], lbac[:, 1, n:n + 1], None, ALU.add)
                        link(ins)
                        for m in range(HEADS):
                            n = d * HEADS + m
                            ins = dve.tensor_scalar(wlv[0][:, m, :], wlv[1][:, m, :], lbac[:, 0, n:n + 1], None, ALU.subtract)
                        ins.then_inc(bound_gap_ready.sem, 1)
                        dve.wait_ge(*bound_log_ready.at(L, d + 1))
                        for m in range(HEADS):
                            n = d * HEADS + m
                            ins = dve.scalar_tensor_tensor(wlv[1][:, m, :], wlv[1][:, m, :], lbac[:, 0, n:n + 1],
                                                           wlv[0][:, m, :], ALU.max, ALU.add)
                        link(ins)
                    for m in range(HEADS):
                        for t in range(NT):
                            o, a = cum[d][:, m, tk(t)], wlv[1][:, m, tk(t)]
                            if d:
                                o, a = o[:, ::-1], a[:, ::-1]
                            ins = dve.tensor_tensor_scan(o, ones, a, 0.0, ALU.mult, ALU.add)
                    ins.then_inc(decay_scanned.sem, 1)

                def halves(ap, half):
                    return ap[:, :, q0:TOKENS].rearrange("p h (b c m) -> p c h b m", c=2, m=half)

                def gap(j):
                    d, lv = (j - 1) // LEVELS, (j - 1) % LEVELS
                    half = P >> (lv + 1)
                    if j >= 2:
                        dve.wait_ge(*level_scored.at(L, j - 1))
                    b, w = halves(cum[d], half), halves(wlv[j % 2], half)
                    shape = [P, HEADS, nq // (2 * half), half]
                    ref = b[:, d][:, :, :, half - 1 if d == 0 else 0:half if d == 0 else 1].broadcast_to(shape)
                    if d == 0:
                        dve.tensor_tensor(w[:, 0], ref, b[:, 0], ALU.subtract)
                        ins = dve.tensor_tensor(w[:, 1], b[:, 1], ref, ALU.subtract)
                    else:
                        dve.tensor_tensor(w[:, 0], b[:, 0], ref, ALU.subtract)
                        ins = dve.tensor_tensor(w[:, 1], ref, b[:, 1], ALU.subtract)
                    ins.then_inc(level_gap.sem, 1)

                def weigh(j):
                    d, lv = (j - 1) // LEVELS, (j - 1) % LEVELS
                    half = P >> (lv + 1)
                    w, q, k = halves(wlv[j % 2], half), halves(qf, half), halves(kg[d], half)
                    dve.wait_ge(*level_exp.at(L, j))
                    dve.tensor_tensor(w[:, d], w[:, d], k[:, d], ALU.mult)
                    dve.tensor_tensor(w[:, 1 - d], w[:, 1 - d], q[:, 1 - d], ALU.mult).then_inc(level_ready.sem, 1)

                def keep(j):
                    dve.wait_ge(*level_scored.at(L, j + 1))
                    if j:
                        dve.wait_ge(*level_kept.at(L, j))
                    for t in tiles:
                        src = ps[:, t, :].rearrange("p (h n) -> p h n", h=HEADS)
                        if j == 0:
                            ins = dve.tensor_copy(amat[:, t], src)
                        else:
                            m = msk[:, (j - 1) // LEVELS, (j - 1) % LEVELS, :].unsqueeze(1).broadcast_to([P, HEADS, P])
                            ins = dve.copy_predicated(amat[:, t], m, src)
                    ins.then_inc(level_kept.sem, 1)

                dve.wait_ge(*key_ready.at(L, 2))
                dve.wait_ge(y_cleared, 16)
                dve.wait_ge(*decay_scanned.at(L, 2))
                dve.wait_ge(*projection_evacuated.at(L, 12))
                dve.tensor_tensor(wlv[0][:, :, q0:TOKENS], kg[0][:, :, q0:TOKENS], kg[1][:, :, q0:TOKENS],
                                  ALU.add).then_inc(level_ready.sem, 1)
                for j in range(1 + 2 * LEVELS):
                    if j < 2 * LEVELS:
                        gap(j + 1)
                    if j:
                        keep(j - 1)
                    if j < 2 * LEVELS:
                        weigh(j + 1)
                keep(2 * LEVELS)

                for d in range(2):
                    b = cum[d].rearrange("p h (t n) -> p (h t) n", n=P)
                    ref = b[:, :, P - 1 if d == 0 else 0:P if d == 0 else 1].broadcast_to([P, 16, P])
                    dve.tensor_tensor(wlv[d].rearrange("p h (t n) -> p (h t) n", n=P), ref, b, ALU.subtract).then_inc(state_gap.sem, 1)
                for d in range(2):
                    dve.wait_ge(*state_exp.at(L, d + 1))
                    dve.tensor_tensor(kg[d], kg[d], wlv[d], ALU.mult).then_inc(state_operands_ready.sem, 1)
                for d in range(2):
                    w = cum[d][:, :, q0:TOKENS]
                    dve.tensor_tensor(w, w, qf[:, :, q0:TOKENS], ALU.mult).then_inc(state_operands_ready.sem, 1)
                dve.wait_ge(*state_operands_ready.at(L, 4))
                for u, (d, t) in enumerate(UPDATES):
                    dve.wait_ge(*state_summed.at(L, u + 1))
                    src = BEFORE[(d, t)]
                    if src is not None:
                        dve.wait_ge(*state_kept.at(L, src + 1))
                    for m in range(HEADS):
                        if src is None:
                            ins = dve.tensor_copy(states[:, u, m, :], ps[:, 6 + u % 2, tk(m)])
                        else:
                            ins = dve.scalar_tensor_tensor(states[:, u, m, :], states[:, src, m, :],
                                                           eb[:, d, m * NT + t:m * NT + t + 1],
                                                           ps[:, 6 + u % 2, tk(m)], ALU.mult, ALU.add)
                    ins.then_inc(state_kept.sem, 1)

                dve.wait_ge(*head_gate_ready.at(L, 1))
                dve.wait_ge(*gain_rows_in.at(L, 48))
                for t in tiles:
                    link(dve.tensor_tensor(gz[:, t, :], gz[:, t, :], ng, ALU.mult))
                dve.wait_ge(*mix_squares.at(L, 1))
                if t0:
                    link(dve.memset(hst[:, 1, 0:4 * t0], 1.0))
                dve.tensor_scalar(hst[:, 1, 4 * t0:], hst[:, 0, 4 * t0:], 1.0 / P, EPS * P, ALU.mult, ALU.add).then_inc(mix_mean.sem, 1)
                for t in tiles:
                    link(dve.tensor_tensor(gz[:, t, :], ps[:, t, :], gz[:, t, :], ALU.mult))
                dve.wait_ge(*mix_root.at(L, 1))
                link(dve.reciprocal(hst[:, 3, :], hst[:, 2, :]))
                for t in tiles:
                    g3 = gz[:, t, :].rearrange("p (h n) -> p h n", h=HEADS)
                    dve.tensor_tensor(g3, g3, bc(hst[:, 3, 4 * t:4 * t + 4], [P, HEADS, P]), ALU.mult).then_inc(mix_ready.sem, 1)

                dve.wait_ge(*qk_root.at(L, 1))
                dve.reciprocal(qst[:, 3, :], qst[:, 2, :]).then_inc(qk_inverse_ready.sem, 1)

                steps = nt * B_HEADS
                for i in range(steps + 2):
                    if i < steps:
                        nk = (LAT0 if tiles[i // B_HEADS] < LAT0 else NT) * P
                        dve.wait_ge(*scores_done.at(L, i + 1))
                        link(dve.reduce_max(mxs[:, 0, i:i + 1], ps[:, 4 + i % 2, 0:nk], AX.X))
                        dve.tensor_scalar(mxs[:, 1, i:i + 1], mxs[:, 0, i:i + 1], -(HD ** -0.5), None, ALU.mult).then_inc(scores_max.sem, 1)
                    n = i - 1
                    if 0 <= n < steps:
                        nk = (LAT0 if tiles[n // B_HEADS] < LAT0 else NT) * P
                        dve.wait_ge(*probs_turned.at(L, n + 1))
                        if n >= 2:
                            dve.wait_ge(*attended.at(L, n - 1))
                        dve.tensor_copy(probsT[:, n % 2, 0:nk], ps[:, 6 + n % 2, 0:nk]).then_inc(probs_copied.sem, 1)
                    n = i - 2
                    if n >= 0 and n % B_HEADS == B_HEADS - 1:
                        k = n // B_HEADS
                        t = tiles[k]
                        dve.wait_ge(*attended.at(L, n + 1))
                        r = mxs[:, 0, k * B_HEADS:(k + 1) * B_HEADS]
                        link(dve.reciprocal(r, mxs[:, 2, k * B_HEADS:(k + 1) * B_HEADS]))
                        dve.tensor_tensor(bq[:, t, :].rearrange("p (h n) -> p h n", h=B_HEADS),
                                          ps[:, k % 2, :].rearrange("p (h n) -> p h n", h=B_HEADS),
                                          bc(r, [P, B_HEADS, HD]), ALU.mult).then_inc(attn_ready.sem, 1)

                for n in range(2 * KD):
                    m = n % KD
                    dve.wait_ge(*merge_sigmoid.at(L, n + 1))
                    dve.wait_ge(*branch_done.at(L, n + 1))
                    s_, u_ = sgm[:, n % 2, 0:nq], ps[:, 6 + n % 2, 0:nq]
                    if n < KD:
                        dve.tensor_tensor(mT[:, m, q0:TOKENS], s_, u_, ALU.mult).then_inc(merged.sem, 1)
                    else:
                        link(dve.tensor_tensor(s_, s_, u_, ALU.mult))
                        dve.tensor_tensor(mT[:, m, q0:TOKENS], mT[:, m, q0:TOKENS], s_, ALU.add).then_inc(merged.sem, 1)
                dve.wait_ge(*gate1_in.at(L, 32))
                n = 0
                for half in range(2):
                    for t in tiles:
                        c0 = slice(half * 512, (half + 1) * 512)
                        dve.wait_ge(*residual_done.at(L, n + 1))
                        if n >= 2:
                            dve.wait_ge(*residual_added.at(L, n - 1))
                        r = sgm[:, n % 2, :]
                        link(dve.tensor_tensor(r, ps[:, n % 4, :], g1b[:, stream(t), c0], ALU.mult))
                        dve.tensor_tensor(h[:, t, c0], h[:, t, c0], r, ALU.add).then_inc(residual_added.sem, 1)
                        n += 1
                dve.wait_ge(*residual_added.at(L, n))
                norm_rows(L, 1, tiles, mod2_in)

                def rt(j):
                    return one[:, j, 0:nt]

                def first_of(dst, values, best, rev, groups, work):
                    w = [P, nt, groups]
                    link(dve.tensor_tensor(dst, values, bc(best, w), ALU.is_equal))
                    r = rev.unsqueeze(1).broadcast_to(w)
                    link(dve.tensor_tensor(dst, dst, r, ALU.mult))
                    link(dve.tensor_reduce(work, dst, AX.X, ALU.max))
                    link(dve.tensor_tensor(dst, r, bc(work, w), ALU.is_equal))

                lgv = lg[:, 0:nt, :]
                dve.wait_ge(*router_in.at(L, 64))
                dve.wait_ge(*logits_done.at(L, 1))
                link(dve.tensor_tensor(lgv, ps[:, 4, 0:nt * 36].rearrange("p (t n) -> p t n", t=nt),
                                       rb.unsqueeze(1).broadcast_to([P, nt, 36]), ALU.add))
                gl = lgv[:, :, 0:NG]
                link(dve.tensor_reduce(rt(0), gl, AX.X, ALU.max))
                goh = grp[:, 0, 0:nt, :]
                first_of(goh, gl, rt(0), cst[:, C_RG:C_RG + NG], NG, rt(1))
                link(dve.tensor_tensor(grp[:, 1, 0:nt, :], gl, bc(rt(0), [P, nt, NG]), ALU.subtract))
                pen = grp[:, 3, 0:nt, :]
                link(dve.tensor_scalar(pen, goh, -1.0, BIG, ALU.add, ALU.mult))
                for i in range(nt):
                    ins = dve.tensor_tensor(em[:, i, :].rearrange("p (g e) -> p g e", g=NG),
                                            lgv[:, i, NG:].rearrange("p (g e) -> p g e", g=NG),
                                            bc(pen[:, i, :], [P, NG, EPG]), ALU.add)
                link(ins)
                e1, e2 = em[:, 0:nt, :], em2[:, 0:nt, :]
                o1, o2 = oh[:, 0, 0:nt, :], oh[:, 1, 0:nt, :]
                rev = cst[:, C_REV:C_REV + NE]
                link(dve.tensor_reduce(rt(2), e1, AX.X, ALU.max))
                first_of(o1, e1, rt(2), rev, NE, rt(1))
                link(dve.scalar_tensor_tensor(e2, o1, -3.0 * BIG, e1, ALU.mult, ALU.add))
                link(dve.tensor_reduce(rt(3), e2, AX.X, ALU.max))
                first_of(o2, e2, rt(3), rev, NE, rt(1))
                dve.tensor_tensor(rt(4), rt(3), rt(2), ALU.subtract).then_inc(route_pre.sem, 1)
                dve.tensor_tensor(both[:, 0:nt, :], o1, o2, ALU.add).then_inc(choices_ready.sem, 1)
                dve.wait_ge(*route_exp.at(L, 1))
                link(dve.tensor_reduce(rt(6), grp[:, 2, 0:nt, :], AX.X, ALU.add))
                link(dve.tensor_scalar(rt(7), rt(5), 1.0, None, ALU.add))
                link(dve.tensor_tensor(rt(6), rt(6), rt(7), ALU.mult))
                link(dve.reciprocal(rt(8), rt(6)))
                link(dve.tensor_tensor(rt(9), rt(8), rt(5), ALU.mult))
                dve.wait_ge(*ranks_done.at(L, 1))
                rk, bk = rank[:, 0:nt, :], nbk[:, 0:nt, :]
                dve.tensor_copy(rk, ps[:, 5, 0:nt * NE].rearrange("p (t n) -> p t n", t=nt))
                link(dve.tensor_copy(cnt[:, 0, :], ps[:, 5, nt * NE:(nt + 1) * NE]))
                dve.tensor_scalar(bk, rk, float(CAP), None, ALU.is_ge)
                link(dve.tensor_scalar(cnt[:, 1, :], cnt[:, 0, :], float(CAP), None, ALU.is_gt))
                for b in range(2, nt * P // CAP):
                    dve.scalar_tensor_tensor(bk, rk, float(b * CAP), bk, ALU.is_ge, ALU.add)
                    link(dve.scalar_tensor_tensor(cnt[:, 1, :], cnt[:, 0, :], float(b * CAP), cnt[:, 1, :], ALU.is_gt, ALU.add))
                link(dve.tensor_tensor_scan(cnt[:, 2, :], ones[:, 0:NE], cnt[:, 1, :], 0.0, ALU.mult, ALU.add))
                link(dve.tensor_tensor(cnt[:, 3, :], cnt[:, 2, :], cnt[:, 1, :], ALU.subtract))
                link(dve.scalar_tensor_tensor(rk, bk, -float(CAP), rk, ALU.mult, ALU.add))
                ew = [P, nt, NE]
                iot = cst[:, C_I32:C_I32 + NE].unsqueeze(1).broadcast_to(ew)
                tw = tmpe[:, 0:nt, :]
                link(dve.scalar_tensor_tensor(tw, bk, float(NE - 1), cnt[:, 3, :].unsqueeze(1).broadcast_to(ew), ALU.add, ALU.add))
                link(dve.tensor_tensor(tw, tw, iot, ALU.subtract))
                link(dve.scalar_tensor_tensor(tw, bk, 0.0, tw, ALU.is_gt, ALU.mult))
                link(dve.tensor_tensor(bk, tw, iot, ALU.add))
                for c_ in range(2):
                    for j, src in enumerate((rk, bk)):
                        link(dve.tensor_tensor(tw, oh[:, c_, 0:nt, :], src, ALU.mult))
                        link(dve.tensor_reduce(rowblk[:, j, c_, 0:nt], tw, AX.X, ALU.add))
                for c_ in range(2):
                    link(dve.scalar_tensor_tensor(slotf[:, c_, 0:nt], rowblk[:, 0, c_, 0:nt], float(NB),
                                                  rowblk[:, 1, c_, 0:nt], ALU.mult, ALU.add))
                    link(dve.tensor_copy(tokslot[:, c_, 0:nt], slotf[:, c_, 0:nt]))
                for i in range(nt):
                    for c_ in range(2):
                        j = 2 * i + c_
                        dve.tensor_scalar(ohrow[:, j, :], cst[:, C_I64:C_I64 + CAP], rowblk[:, 0, c_, i:i + 1], None, ALU.is_equal)
                        ins = dve.tensor_scalar(ohblk[:, j, :], cst[:, C_INB:C_INB + NB], rowblk[:, 1, c_, i:i + 1],
                                                cst[:, C_TOK + i:C_TOK + i + 1], ALU.is_equal, ALU.mult)
                ins.then_inc(table_operands_ready.sem, 1)
                ow = [P, OVER, NE]
                link(dve.tensor_tensor(ovf, cst[:, C_I32:C_I32 + OVER].unsqueeze(2).broadcast_to(ow),
                                       cnt[:, 2, :].unsqueeze(1).broadcast_to(ow), ALU.is_ge))
                link(dve.tensor_reduce(ovn[:, 0:OVER], ovf, AX.X, ALU.add))
                link(dve.tensor_copy(ovn[:, OVER:OVER + 1], cnt[:, 2, NE - 1:NE]))
                link(dve.tensor_copy(numi[:], ovn))
                dve.wait_ge(*table_done.at(L, 1))
                link(dve.tensor_scalar(idxf[0:CAP, 0, :], ps[0:CAP, 6, 0:NB], 0.0, 1e6, ALU.is_equal, ALU.mult))
                link(dve.scalar_tensor_tensor(idxf[0:CAP, 1, :], ps[0:CAP, 6, 0:NB], -1.0, idxf[0:CAP, 0, :], ALU.add, ALU.add))
                dve.tensor_copy(idx[0:CAP, :], idxf[0:CAP, 1, :]).then_inc(routed.sem, 1)

                def expert(X, b, par, early):
                    dve.wait_ge(*X.at("xg_turned", b + 1))
                    if early >= 2:
                        dve.wait_ge(*X.at("up_done", b - 1))
                    dve.tensor_copy(xgT[:, par], ps[:, 0, :].rearrange("p (k n) -> p k n", k=KD)).then_inc(X.sem("xgT_ready"), 1)
                    dve.wait_ge(*X.at("silu_ready", b + 1))
                    if early >= 2:
                        dve.wait_ge(*X.at("h_turned", b - 1))
                    dve.tensor_tensor(hid[:, par, :], sg[:, par, :], ps[:, 1 + par, DE // 2:DE], ALU.mult).then_inc(X.sem("h_ready"), 1)
                    dve.wait_ge(*X.at("h_turned", b + 1))
                    if early >= 2:
                        dve.wait_ge(*X.at("down_done", b - 1))
                    dve.tensor_copy(hT[:, par].rearrange("p j n -> p (j n)"), ps[:, 3, 0:256]).then_inc(X.sem("hT_ready"), 1)

                for par in range(2):
                    expert(main[L], par, par, par)
                with dve.Fori(1, PAIRS) as i:
                    for par in range(2):
                        expert(main[L], 2 * i + par, par, 2)
                dve.wait_ge(*routed.at(L, 1))
                n_over = dve.value_load(numi[0:1, OVER:OVER + 1], min_val=0, max_val=OVER)
                with dve.If(n_over > 0):
                    with dve.Fori(0, n_over) as j:
                        expert(over[L], j, 0, 0)

                dve.wait_ge(*gate2_in.at(L, 32))
                for i, t in enumerate(tiles):
                    a, b = yg[:, i % 2, 0, :], yg[:, i % 2, 1, :]
                    dve.wait_ge(*y_gathered[i % 2].at(L, 32 * (i // 2 + 1)))
                    link(dve.tensor_scalar(a, a, one[:, 8, i:i + 1], None, ALU.mult))
                    link(dve.scalar_tensor_tensor(a, b, one[:, 9, i:i + 1], a, ALU.mult, ALU.add))
                    link(dve.tensor_tensor(a, a, g2b[:, stream(t), :], ALU.mult))
                    dve.tensor_tensor(h[:, t, :], h[:, t, :], a, ALU.add).then_inc(y_used.sem, 1)
                dve.wait_ge(*y_used.at(L, nt))

            norm_scale(2 * DEPTH)
            dve.wait_ge(fin_in, 16)
            for i, t in enumerate(range(LAT0, NT)):
                dve.scalar_tensor_tensor(xn[0][:, i, :], h[:, t, :], stat[:, 2 * DEPTH, 3, t:t + 1], gbc,
                                         ALU.mult, ALU.mult).then_inc(nrm[2 * DEPTH].sem("ready"), 1)

        @block.gpsimd
        def _(pool):
            counted = [0]

            def link(ins):
                counted[0] += 1
                ins.then_inc(pool_step, 1)
                pool.wait_ge(pool_step, counted[0])

            def row(ap):
                return ap.partition_broadcast(P)

            pool.memset(zeros, 0.0).then_inc(y_clear, 1)
            pool.wait_ge(y_clear, 1)
            pool.dma_start(y_dram[:, NE:, :], zeros[0:CAP, :].unsqueeze(1).broadcast_to([CAP, OVER, D])).then_inc(y_cleared, 16)

            for L in range(DEPTH):
                tiles = tiles_of(L)
                nt = len(tiles)
                if L:
                    pool.wait_ge(*y_used.at(L - 1, NT))
                for m in range(4):
                    for st in range(2):
                        src = b_ada[L].rearrange("(n m c) -> m n c", n=12, m=4)[m:m + 1]
                        pool.dma_start(modR[32 * m + st:32 * m + st + 1], src).then_inc(layer_rows_in.sem, 16)
                pool.wait_ge(*mod_rows_ready.at(L, 1))
                for m in range(4):
                    dst = mod_dram[L].rearrange("s (n m c) -> m s n c", n=12, m=4)[m]
                    pool.dma_start(dst, modR[32 * m:32 * m + 2]).then_inc(mod_stored.sem, 16)
                pool.dma_start(gbc, row(norm1_g[L])).then_inc(mod1_in.sem, 16)
                pool.wait_ge(*mod_stored.at(L, 64))
                for st in range(2):
                    pool.dma_start(ab[0][:, st, 0, :], row(mod_rows[L, st, D:2 * D])).then_inc(mod1_in.sem, 16)
                    pool.dma_start(ab[0][:, st, 1, :], row(mod_rows[L, st, 0:D])).then_inc(mod1_in.sem, 16)
                qk_in = gain_rows_in.sem
                pool.wait_ge(*nrm[2 * L].at("ready", NT))
                pool.dma_start(ng, row(hgrn_norm_g[L])).then_inc(qk_in, 16)
                pool.dma_start(qkg[:, 0, :], row(q_norm_g[L])).then_inc(qk_in, 16)
                pool.dma_start(qkg[:, 1, :], row(k_norm_g[L])).then_inc(qk_in, 16)

                pool.wait_ge(*gain_rows_in.at(L, 48))
                pool.wait_ge(*projection_evacuated.at(L, 12 + NT + 2 * nt + NT))
                sq = qsq
                for t in range(NT):
                    for src, n, c0 in ((bq, B_HEADS, 0), (bkv, B_KV, B_HEADS)):
                        if src is bq and t not in tiles:
                            link(pool.memset(qst[:, 0, t * 10:t * 10 + B_HEADS], 1.0))
                            continue
                        a = src[:, t, 0:n * HD]
                        link(pool.tensor_tensor(sq[:, 0:n * HD], a, a, ALU.mult))
                        s3 = sq[:, 0:n * HD].rearrange("p (h n) -> p h n", h=n)
                        wd = HD // 2
                        while wd > 1:
                            link(pool.tensor_tensor(s3[:, :, 0:wd], s3[:, :, 0:wd], s3[:, :, wd:2 * wd], ALU.add))
                            wd //= 2
                        link(pool.tensor_tensor(qst[:, 0, t * 10 + c0:t * 10 + c0 + n].unsqueeze(2), s3[:, :, 0:1],
                                                s3[:, :, 1:2], ALU.add))
                pool.tensor_scalar(qst[:, 1, :], qst[:, 0, :], 1.0 / HD, EPS, ALU.mult, ALU.add).then_inc(qk_mean.sem, 1)
                pool.wait_ge(*qk_inverse_ready.at(L, 1))
                for t in range(NT):
                    for which, (src, n, c0) in enumerate(((bq, B_HEADS, 0), (bkv, B_KV, B_HEADS))):
                        if src is bq and t not in tiles:
                            continue
                        a = src[:, t, 0:n * HD].rearrange("p (h n) -> p h n", h=n)
                        w = [P, n, HD]
                        r = qst[:, 3, t * 10 + c0:t * 10 + c0 + n]
                        link(pool.tensor_tensor(a, a, r.unsqueeze(2).broadcast_to(w), ALU.mult))
                        link(pool.tensor_tensor(a, a, qkg[:, which, :].unsqueeze(1).broadcast_to(w), ALU.mult))
                        if t >= LAT0:
                            o = HD * (t - LAT0)
                            cs = cst[:, C_COS + o:C_COS + o + HD].unsqueeze(1).broadcast_to(w)
                            s3 = qsq[:, 0:n * HD].rearrange("p (h n) -> p h n", h=n)
                            for hf in range(2):
                                for ax in range(2):
                                    c1 = AXIS * ax + hf * AXIS // 2
                                    c2 = AXIS * ax + (1 - hf) * AXIS // 2
                                    sn = cst[:, C_SIN + o + c1:C_SIN + o + c1 + AXIS // 2].unsqueeze(1).broadcast_to([P, n, AXIS // 2])
                                    ins = pool.tensor_tensor(s3[:, :, c1:c1 + AXIS // 2], a[:, :, c2:c2 + AXIS // 2], sn, ALU.mult)
                            link(ins)
                            link(pool.tensor_tensor(a, a, cs, ALU.mult))
                            link(pool.tensor_tensor(a, a, s3, ALU.add))
                link(pool.memset(qst[:, 0, 0:1], 0.0))
                pool.memset(qst[:, 0, 0:1], 0.0).then_inc(qk_ready.sem, 1)

                pool.wait_ge(*mix_done.at(L, nt))
                for st in range(2):
                    pool.dma_start(g1b[:, st, :], row(mod_rows[L, st, 2 * D:3 * D])).then_inc(gate1_in.sem, 16)
                pool.wait_ge(*attn_turned.at(L, nt))
                for st in range(2):
                    pool.dma_start(ab[1][:, st, 0, :], row(mod_rows[L, st, 4 * D:5 * D])).then_inc(mod2_in.sem, 16)
                    pool.dma_start(ab[1][:, st, 1, :], row(mod_rows[L, st, 3 * D:4 * D])).then_inc(mod2_in.sem, 16)
                pool.dma_start(gbc, row(norm2_g[L])).then_inc(mod2_in.sem, 16)
                pool.wait_ge(*branch_done.at(L, KD))
                pool.dma_start(wr[:, :, 0:NG], w_rg[L].rearrange("(k p) n -> p k n", p=P)).then_inc(router_in.sem, 16)
                pool.dma_start(wr[:, :, NG:], w_re[L].rearrange("(k p) n -> p k n", p=P)).then_inc(router_in.sem, 16)
                pool.dma_start(rb[:, 0:NG], row(b_rg[L])).then_inc(router_in.sem, 16)
                pool.dma_start(rb[:, NG:], row(b_re[L])).then_inc(router_in.sem, 16)
                for i, t in enumerate(tiles):
                    pool.wait_ge(*nrm[2 * L + 1].at("ready", i + 1))
                    pool.dma_start(xs_dram[L][tk(i), :], xn[1][:, i % 2, :]).then_inc(moe_input_stored[i % 2].sem, 16)
                for st in range(2):
                    pool.dma_start(g2b[:, st, :], row(mod_rows[L, st, 5 * D:6 * D])).then_inc(gate2_in.sem, 16)
                if L == DEPTH - 1:
                    pool.dma_start(gbc, row(final_norm_g)).then_inc(fin_in, 16)
                pool.memset(xg[:], 0.0).then_inc(xg_clear, 1)
                pool.wait_ge(xg_clear, L + 1)
                for one_of in moe_input_stored:
                    pool.wait_ge(*one_of.at(L, 8 * nt))
                pool.wait_ge(*routed.at(L, 1))

                def expert(X, b, i, par, early, column):
                    if early >= 2:
                        pool.wait_ge(*X.at("xg_turned", b - 1))
                    pool.tensor_copy(idxc[0:CAP, par:par + 1], idx[0:CAP, column]).then_inc(X.sem("idx_ready"), 1)
                    pool.wait_ge(*X.at("idx_ready", b + 1))
                    alone(pool)
                    pool.indirect_dma_start(xg[0:CAP, par, :], None, xs_dram[L],
                                            bass.IndirectOffsetOnAxis(ap=idxc[0:CAP, par:par + 1], axis=0),
                                            bounds_check=nt * P - 1, oob_is_err=False).then_inc(X.sem(f"xg_in{par}"), 16)

                for par in range(2):
                    expert(main[L], par, 0, par, par, slice(par, par + 1))
                with pool.Fori(1, PAIRS) as i:
                    for par in range(2):
                        expert(main[L], 2 * i + par, i, par, 2, bass.ds(2 * i + par, 1))
                pool.wait_ge(*main[L].at("y_stored0", 32 * PAIRS))
                pool.wait_ge(*main[L].at("y_stored1", 32 * PAIRS))
                n_over = pool.value_load(numi[0:1, OVER:OVER + 1], min_val=0, max_val=OVER)
                with pool.If(n_over > 0):
                    with pool.Fori(0, n_over) as j:
                        expert(over[L], j, j, 0, 0, bass.ds(j + NE, 1))
                        pool.wait_ge(*over[L].at("y_stored0", 32 * j + 32))
                for i, t in enumerate(tiles):
                    if i >= 2:
                        pool.wait_ge(*y_used.at(L, i - 1))
                    for c_ in range(2):
                        pool.indirect_dma_start(yg[:, i % 2, c_, :], None, y_rows,
                                                bass.IndirectOffsetOnAxis(ap=tokslot[:, c_, i:i + 1], axis=0),
                                                bounds_check=CAP * NB - 1, oob_is_err=False).then_inc(y_gathered[i % 2].sem, 16)


INS = ["x", "c", "ctx", "c_ctx", "w_ada", "b_ada", "norm1_g", "norm2_g", "w_in", "lb_logits", "hgrn_norm_g",
       "q_norm_g", "k_norm_g", "w_up_a", "w_up_b", "w_out", "w_router_group", "b_router_group", "w_router_expert",
       "b_router_expert", "w_gate", "w_up", "w_down", "final_norm_g"]


def kernel(**inputs):
    import concourse.bacc as bacc
    from concourse.bass_utils import run_bass_kernel_spmd

    nc = bacc.Bacc("TRN2", target_bir_lowering=False, num_devices=1)
    arrays, args = {}, []
    for name in INS:
        a = np.ascontiguousarray(inputs[name])
        arrays[f"in_{name}"] = a
        args.append(nc.dram_tensor(f"in_{name}", a.shape, mybir.dt.from_np(a.dtype), kind="ExternalInput").ap())
    for name, a in (("consts", float_constants()), ("masks", level_masks())):
        arrays[f"in_{name}"] = a
        args.append(nc.dram_tensor(f"in_{name}", a.shape, mybir.dt.from_np(a.dtype), kind="ExternalInput").ap())
    out = nc.dram_tensor("out", (1, SEQ, D), F32, kind="ExternalOutput").ap()
    program(nc, *args, out)
    r = run_bass_kernel_spmd(nc, [arrays], core_ids=[0])
    return r.results[0]["out"]
```

```python
from contextlib import ExitStack

import numpy as np

import concourse.bass as bass
from concourse import mybir

F32 = mybir.dt.float32
I32 = mybir.dt.int32
U8 = mybir.dt.uint8
ALU = mybir.AluOpType
ACT = mybir.ActivationFunctionType
AX = mybir.AxisListType

P = 128
D = 1024
KD = D // P
DEPTH = 2
SEQ = 256
CTX = 256
NT = (SEQ + CTX) // P
LAT0 = CTX // P
EPS = 1e-6
HEADS = 4
AW = HEADS * P
B_HEADS, B_KV, HD = 8, 2, 64
GROUP = B_HEADS // B_KV
GRID_W = 64
AXIS = HD // 2
NG, EPG = 4, 8
NE = NG * EPG
DE = 512
CAP = 64
TOKENS = NT * P
OVER = 2 * TOKENS // CAP
NB = NE + OVER
LEVELS = 7
BIG = 1e30
SLOT = KD * 512
KB = 256
MIX_SLOTS = 4
EXPERT_SLOTS = ((0, 1, 4), (2, 3, 5))
PAIRS = NE // 2
TINY = 2.0 ** -60

Q0, FF0, FB0, I0, GZ0 = 0, AW, 2 * AW, 3 * AW, 4 * AW
BQ0 = 5 * AW
BKV0 = BQ0 + B_HEADS * HD
Z80 = BKV0 + 2 * B_KV * HD
Z90 = Z80 + D
D_IN = Z90 + D

C_ID, C_UP, C_ONE, C_COS, C_SIN = 0, 128, 256, 384, 512
C_I64, C_INB, C_I32, C_REV, C_RG, C_TOK = 640, 704, 752, 784, 816, 820
C_N = 824


def float_constants():
    a = np.zeros((P, C_N), np.float32)
    a[:, C_ID:C_ID + P] = np.eye(P)
    a[:, C_UP:C_UP + P] = np.triu(np.ones((P, P)), 1)
    a[:, C_ONE:C_ONE + P] = 1.0
    t = np.arange(SEQ)
    inv = (np.float32(10000.0) ** (-np.arange(0, AXIS, 2, dtype=np.float32) / np.float32(AXIS))).astype(np.float32)
    pos = np.stack([(t // GRID_W), (t % GRID_W)], 1).astype(np.float32)
    ang = pos[:, :, None] * inv
    cos, sin = np.cos(ang), np.sin(ang)
    cc = np.stack([cos, cos], 2).reshape(SEQ, HD)
    ss = np.stack([-sin, sin], 2).reshape(SEQ, HD)
    for i in range(SEQ // P):
        a[:, C_COS + i * HD:C_COS + (i + 1) * HD] = cc[i * P:(i + 1) * P]
        a[:, C_SIN + i * HD:C_SIN + (i + 1) * HD] = ss[i * P:(i + 1) * P]
    a[:, C_I64:C_I64 + CAP] = np.arange(CAP)
    a[:, C_INB:C_INB + NB] = np.arange(NB)
    a[:, C_I32:C_I32 + NE] = np.arange(NE)
    a[:, C_REV:C_REV + NE] = NE - np.arange(NE)
    a[:, C_RG:C_RG + NG] = NG - np.arange(NG)
    a[:, C_TOK:C_TOK + NT] = np.arange(P)[:, None] + P * np.arange(NT) + 1
    return a


def level_masks():
    m = np.zeros((P, 2, LEVELS, P), np.float32)
    i = np.arange(P)
    for lv in range(LEVELS):
        half = P >> (lv + 1)
        same = (i[:, None] // (2 * half)) == (i[None, :] // (2 * half))
        second = (i // half) % 2 == 1
        fwd = same & ~second[:, None] & second[None, :]
        m[:, 0, lv] = fwd
        m[:, 1, lv] = fwd.T
    return m.reshape(P, 2 * LEVELS * P)


class Signal:

    def __init__(self, semaphore, first):
        self.sem, self.first = semaphore, first

    def at(self, layer, value):
        return self.sem, value + layer * self.first


class Family:

    def __init__(self, semaphores, before):
        self.semaphores, self.before = semaphores, before

    def sem(self, name):
        return self.semaphores[name]

    def at(self, name, value):
        return self.semaphores[name], value + self.before[name]


def plan_loads(layer):
    if layer == 0:
        order = ["ada0", "ada1", "ada2", "ada3", "ff", "ada4", "ada5", "fb", "ada6", "ada7", "q", "ada8", "ada9", "i",
                 "ada10", "ada11", "gz", "bq", "bkv"]
    else:
        order = ["ff", "fb", "q", "i", "gz", "bq", "bkv"]
    names = [(n, i % MIX_SLOTS) for i, n in enumerate(order)]
    names += [("up_a", 3), ("z8_0", 0), ("z8_1", 1), ("up_b", 2), ("z9_0", 0), ("z9_1", 1), ("out0", 3), ("out1", 2)]
    if layer < DEPTH - 1:
        names += [(f"next_ada{n}", s) for n, s in enumerate((0, 1, 3, 0, 1, 2, 3, 0, 1, 2, 3, 2))]
    return names


def program(nc, x, c, ctx_in, c_ctx, w_ada, b_ada, norm1_g, norm2_g, w_in, lb_logits, hgrn_norm_g, q_norm_g,
            k_norm_g, w_up_a, w_up_b, w_out, w_rg, b_rg, w_re, b_re, w_gate, w_up, w_down, final_norm_g,
            consts, masks, out):
    mod_dram = nc.dram_tensor("mod_rows", (DEPTH, 2, 6 * D), F32, kind="Internal").ap()
    xs_dram = [nc.dram_tensor(f"moe_inputs_{L}", (TOKENS if L < DEPTH - 1 else SEQ, D), F32, kind="Internal").ap()
               for L in range(DEPTH)]
    y_dram = nc.dram_tensor("expert_outputs", (CAP, NB, D), F32, kind="Internal").ap()
    y_rows = y_dram.rearrange("c b d -> (c b) d")

    uses = [0] * 6
    where = [{} for _ in range(DEPTH)]
    expert_use = []
    tenant = [[None] * MIX_SLOTS for _ in range(DEPTH)]
    for L in range(DEPTH):
        for name, slot in plan_loads(L):
            where[L][name] = (slot, uses[slot], tenant[L][slot])
            uses[slot] += 1
            tenant[L][slot] = name
        expert_use.append(list(uses))
        for s in range(6):
            uses[s] += PAIRS

    with ExitStack() as ctx:
        def sb(name, shape, dt=F32):
            return ctx.enter_context(nc.sbuf_tensor(name, shape, dt))

        def sem(name):
            return ctx.enter_context(nc.semaphore(name))

        def sems(name):
            return [sem(f"{name}_{L}") for L in range(DEPTH)]

        ps = ctx.enter_context(nc.psum_tensor("ps", [P, 8, 512], F32))
        h = sb("h", [P, NT, D])
        xT = sb("xT", [P, KD, TOKENS])
        ring4 = sb("ring4", [P, MIX_SLOTS, SLOT])
        scr = sb("scr", [P, 104 * KB])
        cst = sb("cst", [P, C_N])
        msk = sb("msk", [P, 2, LEVELS, P], U8)
        stat = sb("stat", [P, 5, 4, NT])
        hst = sb("hst", [P, 4, 16])
        qst = sb("qst", [P, 4, NT * 10])
        mxs = sb("mxs", [P, 3, NT * B_HEADS])
        lbt = sb("lbt", [P, 10, 8])
        lbac = sb("lbac", [P, 2, 8])
        eb = sb("eb", [P, 2, 16])
        cin = sb("cin", [P, KD, 2])
        cact = sb("cact", [P, KD, 2])
        qkg = sb("qkg", [P, 2, HD])
        numi = sb("numi", [P, OVER + 1], I32)

        def area(k0, k1):
            return scr[:, int(k0 * KB):int(k1 * KB)]

        v = area(0, 8).rearrange("p (t n) -> p t n", t=NT)
        qf = area(8, 16).rearrange("p (h t) -> p h t", h=HEADS)
        cum = [area(16, 24).rearrange("p (h t) -> p h t", h=HEADS), area(24, 32).rearrange("p (h t) -> p h t", h=HEADS)]
        kg = [area(32, 40).rearrange("p (h t) -> p h t", h=HEADS), area(40, 48).rearrange("p (h t) -> p h t", h=HEADS)]
        amat = area(48, 56).rearrange("p (t h n) -> p t h n", t=NT, h=HEADS)
        zeros = area(48, 52)
        masks_in = area(56, 63)
        wlv = [area(56, 64).rearrange("p (h t) -> p h t", h=HEADS), area(64, 72).rearrange("p (h t) -> p h t", h=HEADS)]
        states = area(56, 68).rearrange("p (i h n) -> p i h n", i=6, h=HEADS)
        gz = area(72, 80).rearrange("p (t n) -> p t n", t=NT)
        bq = area(80, 88).rearrange("p (t n) -> p t n", t=NT)
        bkv = area(88, 92).rearrange("p (t n) -> p t n", t=NT)
        kT = area(92, 96).rearrange("p (h t) -> p h t", h=B_KV)
        kdn = area(96, 100).rearrange("p (b n) -> p b n", b=2)
        gbc = area(12, 16)
        qsq = area(100, 102)
        ng = area(102, 104)
        modR = area(96, 102).rearrange("p (n c) -> p n c", n=12)
        wr = area(8, 8 + KD * 36 / KB).rearrange("p (k n) -> p k n", k=KD)
        rb = area(9.25, 9.25 + 36 / KB)
        aT = area(8, 16).rearrange("p (k t) -> p k t", k=4)
        bT = area(0, 8).rearrange("p (k t) -> p k t", k=4)
        probs = area(24, 28).rearrange("p (b n) -> p b n", b=2)
        probsT = area(28, 32).rearrange("p (b n) -> p b n", b=2)
        qT = area(56, 72).rearrange("p (h t) -> p h t", h=B_HEADS)
        mT = area(32, 48).rearrange("p (k t) -> p k t", k=KD)
        sgm = area(96, 100).rearrange("p (b n) -> p b n", b=2)
        g1b = area(16, 24).rearrange("p (s n) -> p s n", s=2)
        ab = area(80, 96).rearrange("p (s j n) -> p s j n", s=2, j=2)
        xn = [[area(0, 4), area(4, 8)], [area(24, 28), area(28, 32), area(0, 4), area(4, 8)]]
        junk = area(96, 100)
        ring45 = area(48, 80).rearrange("p (s n) -> p s n", s=2)
        xg = area(0, 8).rearrange("p (b n) -> p b n", b=2)
        yb = area(8, 12).rearrange("p (b n) -> p b n", b=2)
        g2b = area(16, 24).rearrange("p (s n) -> p s n", s=2)
        hid = area(44, 46).rearrange("p (b n) -> p b n", b=2)
        xgT = area(24, 28).rearrange("p (b k n) -> p b k n", b=2, k=KD)
        sg = area(28, 30).rearrange("p (b n) -> p b n", b=2)
        hT = area(30, 32).rearrange("p (b j n) -> p b j n", b=2, j=2)
        yg = area(48, 80).rearrange("p (b j n) -> p b j n", b=NT, j=2)
        at = [32 * KB]

        def routing(n, dt=F32):
            a = scr[:, at[0]:at[0] + n]
            at[0] += n
            assert at[0] <= 44 * KB
            return a if dt is F32 else a.bitcast(dt)

        lg = routing(NT * 36).rearrange("p (t n) -> p t n", t=NT)
        grp = routing(NT * 4 * 4).rearrange("p (j t n) -> p j t n", j=4, t=NT)
        one = routing(NT * 12).rearrange("p (j t) -> p j t", j=12)
        em = routing(NT * NE).rearrange("p (t n) -> p t n", t=NT)
        em2 = routing(NT * NE).rearrange("p (t n) -> p t n", t=NT)
        oh = routing(2 * NT * NE).rearrange("p (j t n) -> p j t n", j=2, t=NT)
        tmpe = routing(NT * NE).rearrange("p (t n) -> p t n", t=NT)
        both = routing(NT * NE).rearrange("p (t n) -> p t n", t=NT)
        rank = routing(NT * NE).rearrange("p (t n) -> p t n", t=NT)
        nbk = routing(NT * NE).rearrange("p (t n) -> p t n", t=NT)
        cnt = routing(4 * NE).rearrange("p (j n) -> p j n", j=4)
        rowblk = routing(2 * 2 * NT).rearrange("p (j c t) -> p j c t", j=2, c=2)
        slotf = routing(2 * NT).rearrange("p (c t) -> p c t", c=2)
        tokslot = routing(2 * NT, I32).rearrange("p (c t) -> p c t", c=2)
        ohrow = routing(2 * NT * CAP).rearrange("p (j n) -> p j n", j=2 * NT)
        ohblk = routing(2 * NT * NB).rearrange("p (j n) -> p j n", j=2 * NT)
        idxf = routing(2 * NB).rearrange("p (j n) -> p j n", j=2)
        idx = routing(NB, I32)
        idxc = routing(2, I32)
        ovf = routing(OVER * NE).rearrange("p (j n) -> p j n", j=OVER)
        ovn = routing(OVER + 1)
        R0 = NT * 36
        T0 = R0 + (NT + 1) * NE
        assert T0 + NB <= 512
        MOD_BANKS = [[5, 0, 1], [5, 6, 7]]
        ident = cst[:, C_ID:C_ID + P]
        ones = cst[:, C_ONE:C_ONE + P]

        def slot_ap(s):
            return ring4[:, s, :] if s < MIX_SLOTS else ring45[:, s - MIX_SLOTS, :]

        def slot3(s, k):
            return slot_ap(s).rearrange("p (k n) -> p k n", k=k)

        s_cst, s_h, s_small = sem("constants_in"), sem("h_in"), sem("small_in")
        loaded = [sem(f"slot{s}_loaded") for s in range(6)]
        dve_step, act_step, pool_step = sem("dve_step"), sem("act_step"), sem("pool_step")
        counts = dict(
            layer_rows_in=128, modulation_slice_done=12, mod_rows_ready=2,
            mod_stored=128, mod1_in=80, gate1_in=32, mod2_in=80, gate2_in=32, router_in=64, gain_rows_in=48,
            projection_done=28, projection_evacuated=28, softplus_ready=2, key_exponent_ready=2, bound_gap_ready=0,
            bound_log_ready=0, decay_scanned=2, key_ready=2, level_gap=2 * LEVELS, level_exp=2 * LEVELS,
            level_ready=1 + 2 * LEVELS, level_scored=1 + 2 * LEVELS, level_kept=1 + 2 * LEVELS, state_gap=2,
            state_exp=2, state_operands_ready=4, keys_turned=6, keys_copied=6, state_summed=6, state_kept=6,
            head_gate_ready=1, mix_done=NT, mix_squares=1, mix_mean=1, mix_root=1, mix_ready=NT, mix_turned=NT,
            mix_copied=NT, qk_mean=1, qk_root=1, qk_inverse_ready=1, qk_ready=1, qk_turned=2 + 2 * NT,
            qk_copied=2 + 2 * NT, scores_done=NT * B_HEADS, scores_max=NT * B_HEADS, probs_ready=NT * B_HEADS,
            probs_turned=NT * B_HEADS, probs_copied=NT * B_HEADS, attended=NT * B_HEADS, attn_ready=NT,
            attn_turned=NT, attn_copied=NT, merge_gate_done=2 * KD, merge_sigmoid=2 * KD, branch_done=2 * KD,
            merged=2 * KD, residual_done=2 * NT, residual_added=2 * NT,
            moe_input_stored0=8 * NT, moe_input_stored1=8 * NT, logits_done=1,
            route_pre=1, route_exp=1, choices_ready=1, ranks_done=1, table_operands_ready=1, table_done=1,
            routed=1, **{f"y_gathered{i}": 32 for i in range(NT)}, y_used=NT, y_scaled=NT)
        signal = {n: Signal(sem(n), k) for n, k in counts.items()}
        layer_rows_in, modulation_slice_done = signal["layer_rows_in"], signal["modulation_slice_done"]
        mod_rows_ready, mod_stored, mod1_in, gate1_in = (signal[n] for n in (
            "mod_rows_ready", "mod_stored", "mod1_in", "gate1_in"))
        mod2_in, gate2_in, router_in, gain_rows_in = (signal[n] for n in (
            "mod2_in", "gate2_in", "router_in", "gain_rows_in"))
        projection_done, projection_evacuated, softplus_ready, key_exponent_ready = (signal[n] for n in (
            "projection_done", "projection_evacuated", "softplus_ready", "key_exponent_ready"))
        bound_gap_ready, bound_log_ready, decay_scanned, key_ready = (signal[n] for n in (
            "bound_gap_ready", "bound_log_ready", "decay_scanned", "key_ready"))
        level_gap, level_exp, level_ready, level_scored = (signal[n] for n in (
            "level_gap", "level_exp", "level_ready", "level_scored"))
        level_kept, state_gap, state_exp, state_operands_ready = (signal[n] for n in (
            "level_kept", "state_gap", "state_exp", "state_operands_ready"))
        keys_turned, keys_copied, state_summed, state_kept = (signal[n] for n in (
            "keys_turned", "keys_copied", "state_summed", "state_kept"))
        head_gate_ready, mix_done, mix_squares, mix_mean = (signal[n] for n in (
            "head_gate_ready", "mix_done", "mix_squares", "mix_mean"))
        mix_root, mix_ready, mix_turned, mix_copied = (signal[n] for n in (
            "mix_root", "mix_ready", "mix_turned", "mix_copied"))
        qk_mean, qk_root, qk_inverse_ready, qk_ready = (signal[n] for n in (
            "qk_mean", "qk_root", "qk_inverse_ready", "qk_ready"))
        qk_turned, qk_copied, scores_done, scores_max = (signal[n] for n in (
            "qk_turned", "qk_copied", "scores_done", "scores_max"))
        probs_ready, probs_turned, probs_copied, attended = (signal[n] for n in (
            "probs_ready", "probs_turned", "probs_copied", "attended"))
        attn_ready, attn_turned, attn_copied, merge_gate_done = (signal[n] for n in (
            "attn_ready", "attn_turned", "attn_copied", "merge_gate_done"))
        merge_sigmoid, branch_done, merged, residual_done = (signal[n] for n in (
            "merge_sigmoid", "branch_done", "merged", "residual_done"))
        residual_added, logits_done, route_pre = (signal[n] for n in (
            "residual_added", "logits_done", "route_pre"))
        route_exp, choices_ready, ranks_done, table_operands_ready = (signal[n] for n in (
            "route_exp", "choices_ready", "ranks_done", "table_operands_ready"))
        table_done, routed, y_used, y_scaled = (signal[n] for n in (
            "table_done", "routed", "y_used", "y_scaled"))
        moe_input_stored = [signal["moe_input_stored0"], signal["moe_input_stored1"]]
        y_gathered = [signal[f"y_gathered{i}"] for i in range(NT)]
        fin_in = sem("final_gain_in")
        cact_ready, lb_ready = sem("conditioning_ready"), sem("bounds_ready")
        lb_exp, lb_pre = sem("bounds_exp"), sem("bounds_pre")
        zeros_ready, y_cleared = sem("zeros_ready"), sem("outputs_cleared")
        xg_clear = sem("gather_buffers_cleared")
        norm_tiles = [NT, NT, NT, NT - LAT0, NT - LAT0]
        norm_sems = {n: sem(f"norm_{n}") for n in ("squares", "mean", "root", "ready", "turned", "copied")}
        nrm = [Family(norm_sems, {n: i for n in ("squares", "mean", "root")} |
                      {n: sum(norm_tiles[:i]) for n in ("ready", "turned", "copied")}) for i in range(2 * DEPTH + 1)]
        moe_names = ["idx_ready", "xg_in0", "xg_in1", "xg_turned", "xgT_ready", "up_done", "silu_ready",
                     "h_ready", "h_turned", "hT_ready", "down_done", "y_copied", "y_stored0", "y_stored1"]
        first_counts = {n: {"xg_in": 16 * PAIRS, "y_stored": 32 * PAIRS}.get(n[:-1], NE) for n in moe_names}
        main_sems = {n: sem(f"expert_{n}") for n in moe_names}
        main = [Family(main_sems, {n: L * first_counts[n] for n in moe_names}) for L in range(DEPTH)]
        over_names = [n for n in moe_names if n[-1] != "1"] + ["loaded"]
        over = [Family({n: sem(f"over_{n}_{L}") for n in over_names}, {n: 0 for n in over_names})
                for L in range(DEPTH)]
        out_done = sem("out_stored")
        passed = sem("waits_passed")

        def block_rows(L):
            return CAP * len(tiles_of(L)) // NT

        def tiles_of(L):
            return list(range(NT)) if L < DEPTH - 1 else list(range(LAT0, NT))

        def stream(tile):
            return 0 if tile < LAT0 else 1

        def tk(tile):
            return slice(tile * P, (tile + 1) * P)

        def sections(L):
            return [("gz", tiles_of(L)), ("bq", tiles_of(L)), ("bkv", list(range(NT)))]

        def release(L, name):
            nt = len(tiles_of(L))
            ends = {"ff": 4, "fb": 8, "q": 12, "i": 12 + NT}
            ends["gz"] = ends["i"] + nt
            ends["bq"] = ends["gz"] + nt
            ends["bkv"] = ends["bq"] + NT
            if name.startswith("ada"):
                return modulation_slice_done.at(L, int(name[3:]) + 1)
            if name.startswith("next_ada"):
                return modulation_slice_done.at(L + 1, int(name[8:]) + 1)
            if name in ends:
                return projection_done.at(L, ends[name])
            z = {"z8_0": 4, "z8_1": 8, "z9_0": 12, "z9_1": 16}
            if name in z:
                return merge_gate_done.at(L, z[name])
            if name in ("up_a", "up_b"):
                return branch_done.at(L, 8 if name == "up_a" else 16)
            return residual_done.at(L, nt if name == "out0" else 2 * nt)

        def level_bank(L, j):
            if L == DEPTH - 1:
                return -LAT0 * (j % 2)
            return NT if j == 2 * LEVELS - 1 else 0

        def level_bank_before(L, j):
            same = [i for i in range(j) if level_bank(L, i) == level_bank(L, j)]
            return same[-1] if same else None

        def schedule(L):
            units = [("unit", n, t) for n, ts in sections(L) for t in ts]
            steps = [("step", j) for j in range(1 + 2 * LEVELS)]
            sched = []
            while units or steps:
                if units:
                    sched.append(units.pop(0))
                if steps:
                    sched.append(steps.pop(0))
            return sched

        UPDATES = [(0, 0), (1, 1), (0, 1), (1, 0), (0, 2), (1, 3)]
        BEFORE = {(0, 0): None, (1, 1): None, (0, 1): 0, (1, 0): 1, (0, 2): 2, (1, 3): 3}
        ENTER = [{1: 0, 2: 2, 3: 4}, {0: 1, 3: 3, 2: 5}]

        block = ctx.enter_context(nc.Block())

        def alone(eng):
            eng.sem_inc(passed)

        @block.sync
        def _(sp):
            sp.dma_start(cst[:], consts).then_inc(s_cst, 16)
            sp.dma_start(masks_in, masks).then_inc(s_cst, 16)
            for st, src in enumerate((c_ctx.rearrange("(k p) -> p k", p=P), c.rearrange("o (k p) -> p (o k)", p=P))):
                sp.dma_start(cin[:, :, st], src, allow_slow_non_contiguous=True).then_inc(s_small, 16)
            for l_ in range(DEPTH):
                for d in range(2):
                    sp.dma_start(lbt[:, l_, d * HEADS:(d + 1) * HEADS], lb_logits[d, l_].rearrange("(h p) -> p h", p=P),
                                 allow_slow_non_contiguous=True).then_inc(s_small, 16)

            def load_tokens():
                for t in range(NT):
                    src = ctx_in[0, tk(t), :] if t < LAT0 else x[0, (t - LAT0) * P:(t - LAT0 + 1) * P, :]
                    sp.dma_start(h[:, t, :], src).then_inc(s_h, 16)

            def w_source(L, name):
                if name.startswith("next_ada"):
                    return w_source(L + 1, name[5:])
                if name.startswith("ada"):
                    n = int(name[3:])
                    return w_ada[L][:, n * 512:(n + 1) * 512].rearrange("(k p) n -> p k n", p=P), KD
                cols = {"q": (Q0, AW), "ff": (FF0, AW), "fb": (FB0, AW), "i": (I0, AW), "gz": (GZ0, AW), "bq": (BQ0, AW),
                        "bkv": (BKV0, Z80 - BKV0), "z8_0": (Z80, 512), "z8_1": (Z80 + 512, 512), "z9_0": (Z90, 512),
                        "z9_1": (Z90 + 512, 512)}
                if name in cols:
                    a, n = cols[name]
                    return w_in[L][:, a:a + n].rearrange("(k p) n -> p k n", p=P), KD
                if name in ("up_a", "up_b"):
                    return (w_up_a if name == "up_a" else w_up_b)[L].rearrange("(k p) n -> p k n", p=P), 4
                n = int(name[3:])
                return w_out[L][:, n * 512:(n + 1) * 512].rearrange("(k p) n -> p k n", p=P), KD

            for L in range(DEPTH):
                experts = [w_gate[L].rearrange("e (k p) n -> p e k n", p=P), w_up[L].rearrange("e (k p) n -> p e k n", p=P),
                           w_down[L].rearrange("e (k p) n -> p e k n", p=P)]
                done = ("up_done", "up_done", "down_done")
                for name, (slot, use, last) in where[L].items():
                    if name == "z9_0":
                        sp.wait_ge(*attn_turned.at(L, len(tiles_of(L))))
                        for par in range(2):
                            s = EXPERT_SLOTS[par][2]
                            sp.dma_start(slot3(s, 4), experts[2][:, par]).then_inc(loaded[s], 16)
                    if L == 0 and name == "ff":
                        load_tokens()
                    if L == 0 and name == "ada4":
                        sp.wait_ge(*mod1_in.at(0, 80))
                    if last:
                        sp.wait_ge(*release(L, last))
                    elif L:
                        sp.wait_ge(*main[L - 1].at("up_done", NE if slot >= 2 else NE - 1))
                        if slot >= 2:
                            sp.wait_ge(*y_gathered[NT - 1].at(L - 1, 32))
                    src, k = w_source(L, name)
                    n = src.shape[-1]
                    dst = slot_ap(slot)[:, 0:k * n].rearrange("p (k n) -> p k n", k=k)
                    sp.dma_start(dst, src).then_inc(loaded[slot], 16)

                def fetch_pair(i, first):
                    for par in range(2):
                        for j in range(3):
                            s = EXPERT_SLOTS[par][j]
                            e = 2 * i + par
                            if first:
                                if s >= MIX_SLOTS:
                                    continue
                                sp.wait_ge(*release(L, tenant[L][s]))
                                src = experts[j][:, e]
                            else:
                                src = experts[j][:, bass.ds(e, 1)].rearrange("p o k n -> p (o k) n")
                                sp.wait_ge(*main[L].at(done[j], e - 1))
                                alone(sp)
                            sp.dma_start(slot3(s, KD if j < 2 else 4), src).then_inc(loaded[s], 16)

                fetch_pair(0, True)
                with sp.Fori(1, PAIRS) as i:
                    fetch_pair(i, False)
                sp.wait_ge(*routed.at(L, 1))
                n_over = sp.value_load(numi[0:1, OVER:OVER + 1], min_val=0, max_val=OVER)
                with sp.If(n_over > 0):
                    sp.wait_ge(*main[L].at("down_done", NE))
                    with sp.Fori(0, n_over) as j:
                        e = sp.value_load(numi[0:1, bass.ds(j, 1)], min_val=0, max_val=NE - 1)
                        for m in range(3):
                            sp.dma_start(slot3(EXPERT_SLOTS[0][m], KD if m < 2 else 4),
                                         experts[m][:, bass.ds(e, 1)].rearrange("p o k n -> p (o k) n")
                                         ).then_inc(over[L].sem("loaded"), 16)
                        sp.wait_ge(*over[L].at("down_done", j + 1))
                        alone(sp)

            sp.wait_ge(out_done, 16 * (NT - LAT0))

        @block.tensor
        def _(pe):
            pe.wait_ge(s_cst, 32)

            def mm(o, a, b, first, last):
                return pe.matmul(o, a, b, start=first, stop=last)

            def turn_norm(L, which, tiles):
                s = nrm[2 * L + which]
                for i, t in enumerate(tiles):
                    pe.wait_ge(*s.at("ready", i + 1))
                    if i >= 2:
                        pe.wait_ge(*s.at("copied", i - 1))
                    for k in range(KD):
                        ins = pe.transpose(ps[:, 2 * (i % 2) + k // 4, (k % 4) * P:(k % 4 + 1) * P],
                                           xn[which][i % len(xn[which])][:, tk(k)], ident)
                    ins.then_inc(s.sem("turned"), 1)

            for L in range(DEPTH):
                tiles = tiles_of(L)
                q0 = tiles[0] * P
                nq = len(tiles) * P
                nt = len(tiles)
                rows = block_rows(L)

                def take(name):
                    slot, use, _ = where[L][name]
                    pe.wait_ge(loaded[slot], 16 * (use + 1))
                    return slot

                def modulate(of, slices):
                    for n in slices:
                        w = slot3(take(f"ada{n}" if of == L else f"next_ada{n}"), KD)
                        for k in range(KD):
                            for m in range(4):
                                ins = mm(ps[32 * m:32 * m + 2, MOD_BANKS[of][n // 4], tk(n % 4)], cact[:, k, :],
                                         w[:, k, tk(m)], k == 0, k == KD - 1)
                        ins.then_inc(modulation_slice_done.sem, 1)

                if L == 0:
                    pe.wait_ge(cact_ready, 1)
                    modulate(0, range(4))
                pe.wait_ge(*mod_rows_ready.at(L, 1 if L == 0 else 2))
                turn_norm(L, 0, range(NT))

                g = 0
                pe.wait_ge(*nrm[2 * L].at("copied", NT))
                for name in ("ff", "fb", "q"):
                    w = slot3(take(name), KD)
                    a = 0 if name != "q" else q0
                    for m in range(HEADS):
                        if g >= 4:
                            pe.wait_ge(*projection_evacuated.at(L, g - 3))
                        for k in range(KD):
                            ins = mm(ps[:, 4 + g % 4, 0:TOKENS - a], w[:, k, tk(m)], xT[:, k, a:TOKENS], k == 0, k == KD - 1)
                        ins.then_inc(projection_done.sem, 1)
                        g += 1
                    if L == 0:
                        n = 4 + 2 * (g // HEADS - 1)
                        modulate(0, (n, n + 1))

                def natural_unit(name, t):
                    nonlocal g
                    slot, use, _ = where[L][name]
                    n = 512 if name != "bkv" else Z80 - BKV0
                    pe.wait_ge(loaded[slot], 16 * (use + 1))
                    w = slot_ap(slot)[:, 0:KD * n].rearrange("p (k n) -> p k n", k=KD)
                    pe.wait_ge(*projection_evacuated.at(L, g - 3))
                    for k in range(KD):
                        ins = mm(ps[:, 4 + g % 4, 0:n], xT[:, k, tk(t)], w[:, k, :], k == 0, k == KD - 1)
                    ins.then_inc(projection_done.sem, 1)
                    g += 1

                for t in range(NT):
                    natural_unit("i", t)
                if L == 0:
                    modulate(0, (10, 11))
                    pe.wait_ge(*mod_rows_ready.at(0, 2))

                def level_scores(j):
                    pe.wait_ge(*level_ready.at(L, j + 1))
                    before = level_bank_before(L, j)
                    if before is not None:
                        pe.wait_ge(*level_kept.at(L, before + 1))
                    if level_bank(L, j) == NT:
                        pe.wait_ge(*projection_evacuated.at(L, g))
                    w = wlv[j % 2]
                    for t in tiles:
                        for hd in range(HEADS):
                            ins = mm(ps[:, t + level_bank(L, j), tk(hd)], w[:, hd, tk(t)],
                                     (w if j else qf)[:, hd, tk(t)], True, True)
                    ins.then_inc(level_scored.sem, 1)

                for what in schedule(L):
                    if what[0] == "unit":
                        natural_unit(what[1], what[2])
                    else:
                        level_scores(what[1])

                def turn_keys(u):
                    d, t = UPDATES[u]
                    if u >= 2:
                        pe.wait_ge(*keys_copied.at(L, u - 1))
                    for hd in range(HEADS):
                        ins = pe.transpose(ps[:, 4 + u % 2, tk(hd)], kg[d][:, hd, tk(t)], ident)
                    ins.then_inc(keys_turned.sem, 1)

                def mix(t):
                    for hd in range(HEADS):
                        parts = [(amat[:, t, hd, :], v[:, t, tk(hd)])]
                        for d in range(2):
                            if t in ENTER[d]:
                                parts.append((cum[d][:, hd, tk(t)], states[:, ENTER[d][t], hd, :]))
                        for n, (a, b) in enumerate(parts):
                            ins = mm(ps[:, t, tk(hd)], a, b, n == 0, n == len(parts) - 1)
                    ins.then_inc(mix_done.sem, 1)

                pe.wait_ge(*state_operands_ready.at(L, 2))
                pe.wait_ge(*projection_evacuated.at(L, g))
                pe.wait_ge(*level_kept.at(L, 1 + 2 * LEVELS))
                turn_keys(0)
                for u, (d, t) in enumerate(UPDATES):
                    if u + 1 < len(UPDATES):
                        turn_keys(u + 1)
                    pe.wait_ge(*keys_copied.at(L, u + 1))
                    if u >= 2:
                        pe.wait_ge(*state_kept.at(L, u - 1))
                    for hd in range(HEADS):
                        ins = mm(ps[:, 6 + u % 2, tk(hd)], kdn[:, u % 2, tk(hd)], v[:, t, tk(hd)], True, True)
                    ins.then_inc(state_summed.sem, 1)
                    if u in (4, 5) and L < DEPTH - 1:
                        pe.wait_ge(*state_operands_ready.at(L, 4))
                        pe.wait_ge(*state_kept.at(L, 3))
                        mix(u - 4)
                pe.wait_ge(*state_kept.at(L, len(UPDATES)))
                pe.wait_ge(*state_operands_ready.at(L, 4))
                for t in range(LAT0, NT):
                    mix(t)

                pe.wait_ge(*qk_ready.at(L, 1))
                turned = 0
                for kv in range(B_KV):
                    for t in range(NT):
                        ins = pe.transpose(ps[0:HD, 4 + turned % 2, tk(t)], bkv[:, t, kv * HD:(kv + 1) * HD], ident)
                    ins.then_inc(qk_turned.sem, 1)
                    turned += 1
                for t in tiles:
                    for half in range(2):
                        pe.wait_ge(*qk_copied.at(L, turned - 1))
                        for m in range(4):
                            hd = 4 * half + m
                            ins = pe.transpose(ps[0:HD, 4 + turned % 2, tk(m)], bq[:, t, hd * HD:(hd + 1) * HD], ident)
                        ins.then_inc(qk_turned.sem, 1)
                        turned += 1

                steps = [(t, hd) for t in tiles for hd in range(B_HEADS)]
                keys = [(LAT0 if t < LAT0 else NT) for t, _ in steps]
                pe.wait_ge(*qk_copied.at(L, turned))
                for i in range(len(steps) + 2):
                    if i < len(steps):
                        t, hd = steps[i]
                        if i >= 2:
                            pe.wait_ge(*probs_ready.at(L, i - 1))
                        mm(ps[:, 4 + i % 2, 0:keys[i] * P], qT[0:HD, hd, tk(t)], kT[0:HD, hd // GROUP, 0:keys[i] * P],
                           True, True).then_inc(scores_done.sem, 1)
                    if 1 <= i <= len(steps):
                        n = i - 1
                        pe.wait_ge(*probs_ready.at(L, n + 1))
                        if n >= 2:
                            pe.wait_ge(*probs_copied.at(L, n - 1))
                        for kc in range(keys[n]):
                            ins = pe.transpose(ps[:, 6 + n % 2, tk(kc)], probs[:, n % 2, tk(kc)], ident)
                        ins.then_inc(probs_turned.sem, 1)
                    if i >= 2:
                        n = i - 2
                        t, hd = steps[n]
                        pe.wait_ge(*probs_copied.at(L, n + 1))
                        if hd == 0:
                            pe.wait_ge(*mix_ready.at(L, nt))
                            if n >= 2 * B_HEADS:
                                pe.wait_ge(*attn_ready.at(L, n // B_HEADS - 1))
                        for kc in range(keys[n]):
                            ins = mm(ps[:, (n // B_HEADS) % 2, hd * HD:(hd + 1) * HD], probsT[:, n % 2, tk(kc)],
                                     bkv[:, kc, (B_KV + hd // GROUP) * HD:(B_KV + hd // GROUP + 1) * HD],
                                     kc == 0, kc == keys[n] - 1)
                        ins.then_inc(attended.sem, 1)

                for i, t in enumerate(tiles):
                    if i >= 2:
                        pe.wait_ge(*mix_copied.at(L, i - 1))
                    for k in range(4):
                        ins = pe.transpose(ps[:, 2 + i % 2, tk(k)], gz[:, t, tk(k)], ident)
                    ins.then_inc(mix_turned.sem, 1)
                for i, t in enumerate(tiles):
                    pe.wait_ge(*attn_ready.at(L, i + 1))
                    if i >= 2:
                        pe.wait_ge(*attn_copied.at(L, i - 1))
                    for k in range(4):
                        ins = pe.transpose(ps[:, 4 + i % 2, tk(k)], bq[:, t, tk(k)], ident)
                    ins.then_inc(attn_turned.sem, 1)

                pe.wait_ge(*mix_copied.at(L, nt))
                pe.wait_ge(*attn_copied.at(L, nt))
                for ph, (zs, up, br) in enumerate(((("z8_0", "z8_1"), "up_a", aT), (("z9_0", "z9_1"), "up_b", bT))):
                    for m in range(KD):
                        n = ph * KD + m
                        w = slot3(take(zs[m // 4]), KD)
                        if n >= 2:
                            pe.wait_ge(*merge_sigmoid.at(L, n - 1))
                        for k in range(KD):
                            ins = mm(ps[:, 4 + n % 2, 0:nq], w[:, k, tk(m % 4)], xT[:, k, q0:TOKENS], k == 0, k == KD - 1)
                        ins.then_inc(merge_gate_done.sem, 1)
                        w = slot3(take(up), 4)
                        if n >= 2:
                            pe.wait_ge(*merged.at(L, n - 1))
                        for k in range(4):
                            ins = mm(ps[:, 6 + n % 2, 0:nq], w[:, k, tk(m)], br[:, k, q0:TOKENS], k == 0, k == 3)
                        ins.then_inc(branch_done.sem, 1)

                def fill(slices):
                    if L < DEPTH - 1:
                        modulate(L + 1, slices)

                pe.wait_ge(*merged.at(L, 2 * KD))
                n = 0
                for half in range(2):
                    w = slot3(take(f"out{half}"), KD)
                    for t in tiles:
                        if n >= 4:
                            pe.wait_ge(*residual_added.at(L, n - 3))
                        for k in range(KD):
                            ins = mm(ps[:, n % 4, :], mT[:, k, tk(t)], w[:, k, :], k == 0, k == KD - 1)
                        ins.then_inc(residual_done.sem, 1)
                        n += 1
                    fill((0, 1) if half == 0 else (2, 3))

                pe.wait_ge(*residual_added.at(L, n))
                turn_norm(L, 1, tiles)
                fill((4,))
                pe.wait_ge(*nrm[2 * L + 1].at("copied", nt))
                pe.wait_ge(*router_in.at(L, 64))
                for i, t in enumerate(tiles):
                    for k in range(KD):
                        ins = mm(ps[:, 4, i * 36:(i + 1) * 36], xT[:, k, tk(t)], wr[:, k, :], k == 0, k == KD - 1)
                ins.then_inc(logits_done.sem, 1)
                fill((5, 6))
                pe.wait_ge(*choices_ready.at(L, 1))
                for i in range(nt):
                    for j in range(i):
                        mm(ps[:, 4, R0 + i * NE:R0 + (i + 1) * NE], ones, both[:, j, :], j == 0, False)
                    mm(ps[:, 4, R0 + i * NE:R0 + (i + 1) * NE], cst[:, C_UP:C_UP + P], both[:, i, :], i == 0, True)
                for j in range(nt):
                    ins = mm(ps[:, 4, R0 + nt * NE:R0 + (nt + 1) * NE], ones, both[:, j, :], j == 0, j == nt - 1)
                ins.then_inc(ranks_done.sem, 1)
                fill((7, 8, 9))
                pe.wait_ge(*table_operands_ready.at(L, 1))
                for j in range(2 * nt):
                    ins = mm(ps[0:CAP, 4, T0:T0 + NB], ohrow[:, j, :], ohblk[:, j, :], j == 0, j == 2 * nt - 1)
                ins.then_inc(table_done.sem, 1)
                fill((10, 11))

                def expert(X, b, i, par, first, weights_in):
                    pe.wait_ge(*X.at(f"xg_in{par}", 16 * (i + 1)))
                    if not first:
                        pe.wait_ge(*X.at("xgT_ready", b))
                    alone(pe)
                    for k in range(KD):
                        ins = pe.transpose(ps[:, 0, k * CAP:k * CAP + rows], xg[0:rows, par, tk(k)], ident[0:rows, 0:rows])
                    ins.then_inc(X.sem("xg_turned"), 1)
                    pe.wait_ge(*X.at("xgT_ready", b + 1))
                    g_, u_, d_ = EXPERT_SLOTS[par]
                    weights_in(g_, i)
                    weights_in(u_, i)
                    w = ring4[:, g_:g_ + 2, :].rearrange("p s (k n) -> p s k n", k=KD)
                    for k in range(KD):
                        for hf in range(2):
                            ins = mm(ps[CAP * hf:CAP * hf + rows, 1 + par, :].rearrange("p (s n) -> p s n", s=2),
                                     xgT[:, par, k, 0:rows], w[:, :, k, DE // 2 * hf:DE // 2 * (hf + 1)], k == 0, k == KD - 1)
                    ins.then_inc(X.sem("up_done"), 1)
                    pe.wait_ge(*X.at("h_ready", b + 1))
                    for j in range(2):
                        ins = pe.transpose(ps[:, 3, tk(j)], hid[:, par, tk(j)], ident)
                    ins.then_inc(X.sem("h_turned"), 1)
                    pe.wait_ge(*X.at("hT_ready", b + 1))
                    weights_in(d_, i)
                    if not first:
                        pe.wait_ge(*X.at("y_copied", b))
                    w = slot3(d_, 4)
                    for k in range(4):
                        for hf in range(2):
                            ins = mm(ps[CAP * hf:CAP * hf + rows, 4, :],
                                     hT[:, par, k % 2, CAP * (k // 2):CAP * (k // 2) + rows],
                                     w[:, k, 512 * hf:512 * (hf + 1)], k == 0, k == 3)
                    ins.then_inc(X.sem("down_done"), 1)

                def ring_in(s, i):
                    pe.wait_ge(loaded[s], 16 * (expert_use[L][s] + 1) + 16 * i)

                for par in range(2):
                    expert(main[L], par, 0, par, par == 0, ring_in)
                with pe.Fori(1, PAIRS) as i:
                    for par in range(2):
                        expert(main[L], 2 * i + par, i, par, False, ring_in)
                pe.wait_ge(*routed.at(L, 1))
                n_over = pe.value_load(numi[0:1, OVER:OVER + 1], min_val=0, max_val=OVER)
                with pe.If(n_over > 0):
                    pe.wait_ge(*main[L].at("y_copied", NE))
                    with pe.Fori(0, n_over) as j:
                        expert(over[L], j, j, 0, True, lambda s, i: pe.wait_ge(*over[L].at("loaded", 48 * j + 48)))

        @block.scalar
        def _(act):
            counted = [0]

            def link(ins):
                counted[0] += 1
                ins.then_inc(act_step, 1)
                act.wait_ge(act_step, counted[0])

            act.wait_ge(s_cst, 32)
            act.wait_ge(s_small, 96)
            act.activation(cact[:], cin[:], ACT.Silu).then_inc(cact_ready, 1)
            act.wait_ge(lb_pre, 1)
            act.activation(lbt[:, 5:7, :], lbt[:, 3:5, :], ACT.Exp).then_inc(lb_exp, 1)
            act.wait_ge(lb_pre, 2)
            act.activation(lbt[:, 5:7, :], lbt[:, 3:5, :], ACT.Ln).then_inc(lb_exp, 1)

            def norm(n, tiles, ready):
                s = nrm[n]
                link(act.activation(stat[:, n, 2, 0:1], ones[:, 0:1], ACT.Sqrt))
                for i, t in enumerate(tiles):
                    ready(i)
                    ins = act.activation(xn[1][1], h[:, t, :], ACT.Square, accum_out=stat[:, n, 0, t:t + 1])
                    if i < len(tiles) - 1:
                        link(ins)
                ins.then_inc(s.sem("squares"), 1)
                act.wait_ge(*s.at("mean", 1))
                act.activation(stat[:, n, 2, :], stat[:, n, 1, :], ACT.Sqrt).then_inc(s.sem("root"), 1)

            def scale_and_sum(L, i):
                for k in ((0, 1) if i == 0 else (i + 1,)):
                    if k < len(tiles_of(L)):
                        act.wait_ge(*y_gathered[k].at(L, 32))
                        act.mul(yg[:, k, 0, :], yg[:, k, 0, :], one[:, 8, k:k + 1]).then_inc(y_scaled.sem, 1)
                act.wait_ge(*y_used.at(L, i + 1))

            def copy_turned(n, tiles):
                s = nrm[n]
                for i, t in enumerate(tiles):
                    act.wait_ge(*s.at("turned", i + 1))
                    b = 2 * (i % 2)
                    act.copy(xT[:, :, tk(t)], ps[:, b:b + 2, :].rearrange("p b (k n) -> p (b k) n", k=4)).then_inc(s.sem("copied"), 1)

            for L in range(DEPTH):
                tiles = tiles_of(L)
                q0 = tiles[0] * P
                nq = len(tiles) * P
                nt = len(tiles)
                rows = block_rows(L)
                if L == 0:
                    norm(0, range(NT), lambda i: act.wait_ge(s_h, 16 * NT))
                else:
                    norm(2 * L, range(NT), lambda i: scale_and_sum(L - 1, i))
                copy_turned(2 * L, range(NT))

                g = 0
                for d in range(2):
                    for m in range(HEADS):
                        act.wait_ge(*projection_done.at(L, g + 1))
                        if d and m == 0:
                            act.wait_ge(*decay_scanned.at(L, 1))
                        act.copy(wlv[0][:, m, :], ps[:, 4 + g % 4, :])
                        act.activation(wlv[1][:, m, :], ps[:, 4 + g % 4, :], ACT.Abs).then_inc(projection_evacuated.sem, 1)
                        g += 1
                    if d:
                        for m in range(HEADS):
                            act.wait_ge(*projection_done.at(L, g + 1))
                            act.activation(qf[:, m, q0:TOKENS], ps[:, 4 + g % 4, 0:nq],
                                           ACT.Silu).then_inc(projection_evacuated.sem, 1)
                            g += 1
                    act.wait_ge(*projection_evacuated.at(L, g))
                    link(act.activation(wlv[1], wlv[1], ACT.Exp, scale=-1.0))
                    act.activation(wlv[1], wlv[1], ACT.Ln, bias=1.0).then_inc(softplus_ready.sem, 1)
                    act.wait_ge(*key_exponent_ready.at(L, d + 1))
                    for m in range(HEADS):
                        ins = act.activation(kg[d][:, m, :], kg[d][:, m, :], ACT.Exp,
                                             bias=lbac[:, 1, d * HEADS + m:d * HEADS + m + 1] if L else 0.0)
                    ins.then_inc(key_ready.sem, 1)
                    if L:
                        act.wait_ge(*bound_gap_ready.at(L, d + 1))
                        link(act.activation(wlv[0], wlv[0], ACT.Abs))
                        link(act.activation(wlv[0], wlv[0], ACT.Exp, scale=-1.0))
                        act.activation(wlv[0], wlv[0], ACT.Ln, bias=1.0).then_inc(bound_log_ready.sem, 1)

                def unit(name, t):
                    nonlocal g
                    n = 512 if name != "bkv" else Z80 - BKV0
                    act.wait_ge(*projection_done.at(L, g + 1))
                    dst = {"i": v, "gz": gz, "bq": bq, "bkv": bkv}[name]
                    act.copy(dst[:, t, :], ps[:, 4 + g % 4, 0:n]).then_inc(projection_evacuated.sem, 1)
                    g += 1

                for t in range(NT):
                    unit("i", t)
                for what in schedule(L):
                    if what[0] == "unit":
                        unit(what[1], what[2])
                    elif what[1] < 2 * LEVELS:
                        j = what[1] + 1
                        act.wait_ge(*level_gap.at(L, j))
                        w = wlv[j % 2][:, :, q0:TOKENS]
                        act.activation(w, w, ACT.Exp).then_inc(level_exp.sem, 1)

                act.wait_ge(*qk_mean.at(L, 1))
                act.activation(qst[:, 2, :], qst[:, 1, :], ACT.Sqrt).then_inc(qk_root.sem, 1)
                for d in range(2):
                    act.wait_ge(*state_gap.at(L, d + 1))
                    act.activation(wlv[d], wlv[d], ACT.Exp)
                    last = cum[d].rearrange("p h (t n) -> p (h t) n", n=P)[:, :, P - 1 if d == 0 else 0]
                    link(act.activation(eb[:, d, :], last, ACT.Exp))
                    w = cum[d][:, :, q0:TOKENS]
                    act.activation(w, w, ACT.Exp).then_inc(state_exp.sem, 1)
                for u in range(len(UPDATES)):
                    act.wait_ge(*keys_turned.at(L, u + 1))
                    if u >= 2:
                        act.wait_ge(*state_summed.at(L, u - 1))
                    act.copy(kdn[:, u % 2, :], ps[:, 4 + u % 2, :]).then_inc(keys_copied.sem, 1)
                act.wait_ge(*projection_evacuated.at(L, g))
                w = gz[:, tiles[0]:NT, :]
                act.activation(w, w, ACT.Silu).then_inc(head_gate_ready.sem, 1)
                for i, t in enumerate(tiles):
                    act.wait_ge(*mix_done.at(L, i + 1))
                    for hd in range(HEADS):
                        n = 4 * t + hd
                        link(act.activation(junk[:, (n % 8) * P:(n % 8 + 1) * P], ps[:, t, tk(hd)], ACT.Square,
                                            accum_out=hst[:, 0, n:n + 1]))
                act.copy(hst[:, 2, 0:1], hst[:, 0, 4 * tiles[0]:4 * tiles[0] + 1]).then_inc(mix_squares.sem, 1)
                act.wait_ge(*mix_mean.at(L, 1))
                act.activation(hst[:, 2, :], hst[:, 1, :], ACT.Sqrt).then_inc(mix_root.sem, 1)
                turned = 0
                for kv in range(B_KV):
                    act.wait_ge(*qk_turned.at(L, turned + 1))
                    act.copy(kT[0:HD, kv, :], ps[0:HD, 4 + turned % 2, :]).then_inc(qk_copied.sem, 1)
                    turned += 1
                for t in tiles:
                    for half in range(2):
                        act.wait_ge(*qk_turned.at(L, turned + 1))
                        act.copy(qT[0:HD, 4 * half:4 * half + 4, tk(t)],
                                 ps[0:HD, 4 + turned % 2, :].rearrange("p (m n) -> p m n", m=4)).then_inc(qk_copied.sem, 1)
                        turned += 1
                for i in range(nt * B_HEADS):
                    t = tiles[i // B_HEADS]
                    nk = (LAT0 if t < LAT0 else NT) * P
                    act.wait_ge(*scores_max.at(L, i + 1))
                    if i >= 2:
                        act.wait_ge(*probs_turned.at(L, i - 1))
                    act.activation(probs[:, i % 2, 0:nk], ps[:, 4 + i % 2, 0:nk], ACT.Exp, bias=mxs[:, 1, i:i + 1],
                                   scale=HD ** -0.5, accum_out=mxs[:, 2, i:i + 1]).then_inc(probs_ready.sem, 1)
                for i, t in enumerate(tiles):
                    act.wait_ge(*mix_turned.at(L, i + 1))
                    act.copy(aT[:, :, tk(t)], ps[:, 2 + i % 2, :].rearrange("p (k n) -> p k n", k=4)).then_inc(mix_copied.sem, 1)
                for i, t in enumerate(tiles):
                    act.wait_ge(*attn_turned.at(L, i + 1))
                    act.copy(bT[:, :, tk(t)], ps[:, 4 + i % 2, :].rearrange("p (k n) -> p k n", k=4)).then_inc(attn_copied.sem, 1)

                for n in range(2 * KD):
                    act.wait_ge(*merge_gate_done.at(L, n + 1))
                    if n >= 2:
                        act.wait_ge(*merged.at(L, n - 1))
                    act.activation(sgm[:, n % 2, 0:nq], ps[:, 4 + n % 2, 0:nq], ACT.Sigmoid).then_inc(merge_sigmoid.sem, 1)

                norm(2 * L + 1, tiles, lambda i: act.wait_ge(*residual_added.at(L, nt + i + 1)))
                copy_turned(2 * L + 1, tiles)
                act.wait_ge(*route_pre.at(L, 1))
                act.activation(grp[:, 2, 0:nt, :], grp[:, 1, 0:nt, :], ACT.Exp)
                act.activation(one[:, 5, 0:nt], one[:, 4, 0:nt], ACT.Exp).then_inc(route_exp.sem, 1)

                def expert(X, b, i, par, early, column):
                    act.wait_ge(*X.at("up_done", b + 1))
                    if early >= 2:
                        act.wait_ge(*X.at("h_ready", b - 1))
                    act.activation(sg[:, par, :], ps[:, 1 + par, 0:DE // 2], ACT.Silu).then_inc(X.sem("silu_ready"), 1)
                    act.wait_ge(*X.at("down_done", b + 1))
                    if early >= 2:
                        act.wait_ge(*X.at(f"y_stored{par}", 32 * i))
                    act.copy(yb[:, par, :], ps[:, 4, :]).then_inc(X.sem("y_copied"), 1)
                    act.wait_ge(*X.at("y_copied", b + 1))
                    for hf in range(2):
                        dst = y_dram[0:rows, column, 512 * hf:512 * (hf + 1)]
                        if isinstance(column, bass.DynSlice):
                            dst = dst.rearrange("c o n -> c (o n)")
                        act.dma_start(dst, yb[CAP * hf:CAP * hf + rows, par, :]).then_inc(X.sem(f"y_stored{par}"), 16)

                for par in range(2):
                    expert(main[L], par, 0, par, par, par)
                with act.Fori(1, PAIRS) as i:
                    for par in range(2):
                        expert(main[L], 2 * i + par, i, par, 2, bass.ds(2 * i + par, 1))
                act.wait_ge(*routed.at(L, 1))
                n_over = act.value_load(numi[0:1, OVER:OVER + 1], min_val=0, max_val=OVER)
                with act.If(n_over > 0):
                    act.wait_ge(*main[L].at("y_stored0", 32 * PAIRS))
                    act.wait_ge(*main[L].at("y_stored1", 32 * PAIRS))
                    with act.Fori(0, n_over) as j:
                        expert(over[L], j, j, 0, 0, bass.ds(j + NE, 1))

            norm(2 * DEPTH, range(LAT0, NT), lambda i: scale_and_sum(DEPTH - 1, i))
            for i, t in enumerate(range(LAT0, NT)):
                act.wait_ge(*nrm[2 * DEPTH].at("ready", i + 1))
                act.dma_start(out[0, (t - LAT0) * P:(t - LAT0 + 1) * P, :], xn[0][i]).then_inc(out_done, 16)

        @block.vector
        def _(dve):
            counted = [0]

            def link(ins):
                counted[0] += 1
                ins.then_inc(dve_step, 1)
                dve.wait_ge(dve_step, counted[0])

            def bc(ap, shape):
                return ap.unsqueeze(len(ap.shape)).broadcast_to(shape)

            dve.wait_ge(s_small, 96)
            dve.wait_ge(s_cst, 32)
            link(dve.tensor_copy(msk[:].rearrange("p a b n -> p (a b n)"), masks_in))
            link(dve.tensor_tensor(lbt[:, 2, :], lbt[:, 0, :], lbt[:, 1, :], ALU.max))
            dve.tensor_tensor(lbt[:, 3, :], lbt[:, 0, :], lbt[:, 2, :], ALU.subtract)
            dve.tensor_tensor(lbt[:, 4, :], lbt[:, 1, :], lbt[:, 2, :], ALU.subtract).then_inc(lb_pre, 1)
            dve.wait_ge(lb_exp, 1)
            link(dve.tensor_tensor(lbt[:, 7, :], lbt[:, 5, :], lbt[:, 6, :], ALU.add))
            link(dve.reciprocal(lbt[:, 7, :], lbt[:, 7, :]))
            link(dve.tensor_tensor(lbt[:, 8, :], lbt[:, 5, :], lbt[:, 7, :], ALU.mult))
            link(dve.tensor_tensor(lbt[:, 9, :], lbt[:, 6, :], lbt[:, 7, :], ALU.mult))
            link(dve.tensor_tensor(lbt[:, 9, :], lbt[:, 8, :], lbt[:, 9, :], ALU.add))
            link(dve.tensor_tensor(lbt[:, 9, :], lbt[:, 9, :], lbt[:, 8, :], ALU.subtract))
            link(dve.tensor_scalar(lbt[:, 2, :], lbt[:, 9, :], -1.0, 1.0, ALU.mult, ALU.add))
            dve.tensor_scalar(lbt[:, 3, :], lbt[:, 9, :], TINY, None, ALU.max)
            dve.tensor_scalar(lbt[:, 4, :], lbt[:, 2, :], TINY, None, ALU.max).then_inc(lb_pre, 1)
            link(dve.tensor_scalar(lbt[:, 0, :], lbt[:, 9, :], 0.0, -BIG, ALU.is_equal, ALU.mult))
            link(dve.tensor_scalar(lbt[:, 1, :], lbt[:, 2, :], 0.0, -BIG, ALU.is_equal, ALU.mult))
            dve.wait_ge(lb_exp, 2)
            link(dve.tensor_tensor(lbac[:, 0, :], lbt[:, 5, :], lbt[:, 0, :], ALU.add))
            dve.tensor_tensor(lbac[:, 1, :], lbt[:, 6, :], lbt[:, 1, :], ALU.add).then_inc(lb_ready, 1)

            def norm_scale(n):
                s = nrm[n]
                dve.wait_ge(*s.at("squares", 1))
                a = LAT0 if n >= 2 * DEPTH - 1 else 0
                if a:
                    link(dve.memset(stat[:, n, 1, 0:a], 1.0))
                dve.tensor_scalar(stat[:, n, 1, a:], stat[:, n, 0, a:], 1.0 / D, EPS, ALU.mult, ALU.add).then_inc(s.sem("mean"), 1)
                dve.wait_ge(*s.at("root", 1))
                link(dve.reciprocal(stat[:, n, 3, :], stat[:, n, 2, :]))

            def norm_factors(L, tiles, mod_in):
                dve.wait_ge(*mod_in.at(L, 16 * 5))
                for st in range(stream(tiles[0]), 2):
                    link(dve.scalar_tensor_tensor(ab[:, st, 0, :], ab[:, st, 0, :], 1.0, gbc, ALU.add, ALU.mult))

            def norm_rows(L, which, tiles):
                n = 2 * L + which
                s = nrm[n]
                norm_scale(n)
                for i, t in enumerate(tiles):
                    if i >= len(xn[which]):
                        dve.wait_ge(*s.at("turned", i - 1))
                    xx = xn[which][i % len(xn[which])]
                    st = stream(t)
                    link(dve.scalar_tensor_tensor(xx, h[:, t, :], stat[:, n, 3, t:t + 1], ab[:, st, 0, :],
                                                  ALU.mult, ALU.mult))
                    dve.tensor_tensor(xx, xx, ab[:, st, 1, :], ALU.add).then_inc(s.sem("ready"), 1)

            def add_bias(L, thirds):
                dve.wait_ge(*layer_rows_in.at(L, 16 * 8))
                for q_ in thirds:
                    dve.wait_ge(*modulation_slice_done.at(L, 4 * q_ + 4))
                    for m in range(4):
                        r = modR[32 * m:32 * m + 2, 4 * q_:4 * q_ + 4, :]
                        src = ps[32 * m:32 * m + 2, MOD_BANKS[L][q_], :].rearrange("p (n c) -> p n c", n=4)
                        ins = dve.tensor_tensor(r, src, r, ALU.add)
                ins.then_inc(mod_rows_ready.sem, 1)

            for L in range(DEPTH):
                tiles = tiles_of(L)
                t0 = tiles[0]
                q0 = t0 * P
                nq = len(tiles) * P
                nt = len(tiles)
                rows = block_rows(L)
                if L == 0:
                    add_bias(0, (0,))
                    norm_factors(0, list(range(NT)), mod1_in)
                norm_rows(L, 0, list(range(NT)))

                for d in range(2):
                    dve.wait_ge(*softplus_ready.at(L, d + 1))
                    link(dve.scalar_tensor_tensor(wlv[1], wlv[0], 0.0, wlv[1], ALU.min, ALU.subtract))
                    dve.tensor_tensor(kg[d], wlv[1], wlv[0], ALU.subtract).then_inc(key_exponent_ready.sem, 1)
                    if L:
                        if d == 0:
                            dve.wait_ge(lb_ready, 1)
                        dve.wait_ge(*key_exponent_ready.at(L, d + 1))
                        for m in range(HEADS):
                            n = d * HEADS + m
                            ins = dve.tensor_scalar(wlv[1][:, m, :], wlv[1][:, m, :], lbac[:, 1, n:n + 1], None, ALU.add)
                        link(ins)
                        for m in range(HEADS):
                            n = d * HEADS + m
                            ins = dve.tensor_scalar(wlv[0][:, m, :], wlv[1][:, m, :], lbac[:, 0, n:n + 1], None, ALU.subtract)
                        ins.then_inc(bound_gap_ready.sem, 1)
                        dve.wait_ge(*bound_log_ready.at(L, d + 1))
                        for m in range(HEADS):
                            n = d * HEADS + m
                            ins = dve.scalar_tensor_tensor(wlv[1][:, m, :], wlv[1][:, m, :], lbac[:, 0, n:n + 1],
                                                           wlv[0][:, m, :], ALU.max, ALU.add)
                        link(ins)
                    for m in range(HEADS):
                        for t in range(NT):
                            o, a = cum[d][:, m, tk(t)], wlv[1][:, m, tk(t)]
                            if d:
                                o, a = o[:, ::-1], a[:, ::-1]
                            ins = dve.tensor_tensor_scan(o, ones, a, 0.0, ALU.mult, ALU.add)
                    ins.then_inc(decay_scanned.sem, 1)

                if L == 0:
                    add_bias(0, (1, 2))

                def halves(ap, half):
                    return ap[:, :, q0:TOKENS].rearrange("p h (b c m) -> p c h b m", c=2, m=half)

                def gap(j):
                    d, lv = (j - 1) // LEVELS, (j - 1) % LEVELS
                    half = P >> (lv + 1)
                    if j >= 2:
                        dve.wait_ge(*level_scored.at(L, j - 1))
                    b, w = halves(cum[d], half), halves(wlv[j % 2], half)
                    shape = [P, HEADS, nq // (2 * half), half]
                    ref = b[:, d][:, :, :, half - 1 if d == 0 else 0:half if d == 0 else 1].broadcast_to(shape)
                    if d == 0:
                        dve.tensor_tensor(w[:, 0], ref, b[:, 0], ALU.subtract)
                        ins = dve.tensor_tensor(w[:, 1], b[:, 1], ref, ALU.subtract)
                    else:
                        dve.tensor_tensor(w[:, 0], b[:, 0], ref, ALU.subtract)
                        ins = dve.tensor_tensor(w[:, 1], ref, b[:, 1], ALU.subtract)
                    ins.then_inc(level_gap.sem, 1)

                def weigh(j):
                    d, lv = (j - 1) // LEVELS, (j - 1) % LEVELS
                    half = P >> (lv + 1)
                    w, q, k = halves(wlv[j % 2], half), halves(qf, half), halves(kg[d], half)
                    dve.wait_ge(*level_exp.at(L, j))
                    dve.tensor_tensor(w[:, d], w[:, d], k[:, d], ALU.mult)
                    dve.tensor_tensor(w[:, 1 - d], w[:, 1 - d], q[:, 1 - d], ALU.mult).then_inc(level_ready.sem, 1)

                def keep(j):
                    dve.wait_ge(*level_scored.at(L, j + 1))
                    if j:
                        dve.wait_ge(*level_kept.at(L, j))
                    for t in tiles:
                        src = ps[:, t + level_bank(L, j), :].rearrange("p (h n) -> p h n", h=HEADS)
                        if j == 0:
                            ins = dve.tensor_copy(amat[:, t], src)
                        else:
                            m = msk[:, (j - 1) // LEVELS, (j - 1) % LEVELS, :].unsqueeze(1).broadcast_to([P, HEADS, P])
                            ins = dve.copy_predicated(amat[:, t], m, src)
                    ins.then_inc(level_kept.sem, 1)

                dve.wait_ge(*key_ready.at(L, 2))
                dve.wait_ge(y_cleared, 16)
                dve.wait_ge(*decay_scanned.at(L, 2))
                dve.wait_ge(*projection_evacuated.at(L, 12))
                dve.tensor_tensor(wlv[0][:, :, q0:TOKENS], kg[0][:, :, q0:TOKENS], kg[1][:, :, q0:TOKENS],
                                  ALU.add).then_inc(level_ready.sem, 1)
                for j in range(1 + 2 * LEVELS):
                    if j < 2 * LEVELS:
                        gap(j + 1)
                    if j:
                        keep(j - 1)
                    if j < 2 * LEVELS:
                        weigh(j + 1)
                keep(2 * LEVELS)

                for d in range(2):
                    b = cum[d].rearrange("p h (t n) -> p (h t) n", n=P)
                    ref = b[:, :, P - 1 if d == 0 else 0:P if d == 0 else 1].broadcast_to([P, 16, P])
                    dve.tensor_tensor(wlv[d].rearrange("p h (t n) -> p (h t) n", n=P), ref, b,
                                      ALU.subtract).then_inc(state_gap.sem, 1)
                dve.wait_ge(*qk_root.at(L, 1))
                dve.reciprocal(qst[:, 3, :], qst[:, 2, :]).then_inc(qk_inverse_ready.sem, 1)
                for d in range(2):
                    dve.wait_ge(*state_exp.at(L, d + 1))
                    dve.tensor_tensor(kg[d], kg[d], wlv[d], ALU.mult).then_inc(state_operands_ready.sem, 1)
                for d in range(2):
                    w = cum[d][:, :, q0:TOKENS]
                    dve.tensor_tensor(w, w, qf[:, :, q0:TOKENS], ALU.mult).then_inc(state_operands_ready.sem, 1)
                dve.wait_ge(*state_operands_ready.at(L, 4))
                for u, (d, t) in enumerate(UPDATES):
                    dve.wait_ge(*state_summed.at(L, u + 1))
                    src = BEFORE[(d, t)]
                    if src is not None:
                        dve.wait_ge(*state_kept.at(L, src + 1))
                    for m in range(HEADS):
                        if src is None:
                            ins = dve.tensor_copy(states[:, u, m, :], ps[:, 6 + u % 2, tk(m)])
                        else:
                            ins = dve.scalar_tensor_tensor(states[:, u, m, :], states[:, src, m, :],
                                                           eb[:, d, m * NT + t:m * NT + t + 1],
                                                           ps[:, 6 + u % 2, tk(m)], ALU.mult, ALU.add)
                    ins.then_inc(state_kept.sem, 1)

                dve.wait_ge(*head_gate_ready.at(L, 1))
                dve.wait_ge(*gain_rows_in.at(L, 48))
                for t in tiles:
                    link(dve.tensor_tensor(gz[:, t, :], gz[:, t, :], ng, ALU.mult))
                dve.wait_ge(*mix_squares.at(L, 1))
                if t0:
                    link(dve.memset(hst[:, 1, 0:4 * t0], 1.0))
                dve.tensor_scalar(hst[:, 1, 4 * t0:], hst[:, 0, 4 * t0:], 1.0 / P, EPS * P,
                                  ALU.mult, ALU.add).then_inc(mix_mean.sem, 1)
                for t in tiles:
                    link(dve.tensor_tensor(gz[:, t, :], ps[:, t, :], gz[:, t, :], ALU.mult))
                dve.wait_ge(*mix_root.at(L, 1))
                link(dve.reciprocal(hst[:, 3, :], hst[:, 2, :]))
                for t in tiles:
                    g3 = gz[:, t, :].rearrange("p (h n) -> p h n", h=HEADS)
                    dve.tensor_tensor(g3, g3, bc(hst[:, 3, 4 * t:4 * t + 4], [P, HEADS, P]), ALU.mult).then_inc(mix_ready.sem, 1)

                steps = nt * B_HEADS
                for i in range(steps + 2):
                    if i < steps:
                        nk = (LAT0 if tiles[i // B_HEADS] < LAT0 else NT) * P
                        dve.wait_ge(*scores_done.at(L, i + 1))
                        link(dve.reduce_max(mxs[:, 0, i:i + 1], ps[:, 4 + i % 2, 0:nk], AX.X))
                        dve.tensor_scalar(mxs[:, 1, i:i + 1], mxs[:, 0, i:i + 1], -(HD ** -0.5), None,
                                          ALU.mult).then_inc(scores_max.sem, 1)
                    n = i - 1
                    if 0 <= n < steps:
                        nk = (LAT0 if tiles[n // B_HEADS] < LAT0 else NT) * P
                        dve.wait_ge(*probs_turned.at(L, n + 1))
                        if n >= 2:
                            dve.wait_ge(*attended.at(L, n - 1))
                        dve.tensor_copy(probsT[:, n % 2, 0:nk], ps[:, 6 + n % 2, 0:nk]).then_inc(probs_copied.sem, 1)
                    n = i - 2
                    if n >= 0 and n % B_HEADS == B_HEADS - 1:
                        k = n // B_HEADS
                        t = tiles[k]
                        dve.wait_ge(*attended.at(L, n + 1))
                        r = mxs[:, 0, k * B_HEADS:(k + 1) * B_HEADS]
                        link(dve.reciprocal(r, mxs[:, 2, k * B_HEADS:(k + 1) * B_HEADS]))
                        dve.tensor_tensor(bq[:, t, :].rearrange("p (h n) -> p h n", h=B_HEADS),
                                          ps[:, k % 2, :].rearrange("p (h n) -> p h n", h=B_HEADS),
                                          bc(r, [P, B_HEADS, HD]), ALU.mult).then_inc(attn_ready.sem, 1)

                for n in range(2 * KD):
                    m = n % KD
                    dve.wait_ge(*merge_sigmoid.at(L, n + 1))
                    dve.wait_ge(*branch_done.at(L, n + 1))
                    s_, u_ = sgm[:, n % 2, 0:nq], ps[:, 6 + n % 2, 0:nq]
                    if n < KD:
                        dve.tensor_tensor(mT[:, m, q0:TOKENS], s_, u_, ALU.mult).then_inc(merged.sem, 1)
                    else:
                        link(dve.tensor_tensor(s_, s_, u_, ALU.mult))
                        dve.tensor_tensor(mT[:, m, q0:TOKENS], mT[:, m, q0:TOKENS], s_, ALU.add).then_inc(merged.sem, 1)
                norm_factors(L, tiles, mod2_in)
                dve.wait_ge(*gate1_in.at(L, 32))
                n = 0
                for half in range(2):
                    for t in tiles:
                        c0 = slice(half * 512, (half + 1) * 512)
                        dve.wait_ge(*residual_done.at(L, n + 1))
                        if n >= 2:
                            dve.wait_ge(*residual_added.at(L, n - 1))
                        r = sgm[:, n % 2, :]
                        link(dve.tensor_tensor(r, ps[:, n % 4, :], g1b[:, stream(t), c0], ALU.mult))
                        dve.tensor_tensor(h[:, t, c0], h[:, t, c0], r, ALU.add).then_inc(residual_added.sem, 1)
                        n += 1
                dve.wait_ge(*residual_added.at(L, n))
                norm_rows(L, 1, tiles)

                def rt(j):
                    return one[:, j, 0:nt]

                def first_of(dst, values, best, rev, groups, work):
                    w = [P, nt, groups]
                    link(dve.tensor_tensor(dst, values, bc(best, w), ALU.is_equal))
                    r = rev.unsqueeze(1).broadcast_to(w)
                    link(dve.tensor_tensor(dst, dst, r, ALU.mult))
                    link(dve.tensor_reduce(work, dst, AX.X, ALU.max))
                    link(dve.tensor_tensor(dst, r, bc(work, w), ALU.is_equal))

                lgv = lg[:, 0:nt, :]
                dve.wait_ge(*router_in.at(L, 64))
                dve.wait_ge(*logits_done.at(L, 1))
                link(dve.tensor_tensor(lgv, ps[:, 4, 0:nt * 36].rearrange("p (t n) -> p t n", t=nt),
                                       rb.unsqueeze(1).broadcast_to([P, nt, 36]), ALU.add))
                gl = lgv[:, :, 0:NG]
                link(dve.tensor_reduce(rt(0), gl, AX.X, ALU.max))
                goh = grp[:, 0, 0:nt, :]
                first_of(goh, gl, rt(0), cst[:, C_RG:C_RG + NG], NG, rt(1))
                link(dve.tensor_tensor(grp[:, 1, 0:nt, :], gl, bc(rt(0), [P, nt, NG]), ALU.subtract))
                pen = grp[:, 3, 0:nt, :]
                link(dve.tensor_scalar(pen, goh, -1.0, BIG, ALU.add, ALU.mult))
                for i in range(nt):
                    ins = dve.tensor_tensor(em[:, i, :].rearrange("p (g e) -> p g e", g=NG),
                                            lgv[:, i, NG:].rearrange("p (g e) -> p g e", g=NG),
                                            bc(pen[:, i, :], [P, NG, EPG]), ALU.add)
                link(ins)
                e1, e2 = em[:, 0:nt, :], em2[:, 0:nt, :]
                o1, o2 = oh[:, 0, 0:nt, :], oh[:, 1, 0:nt, :]
                rev = cst[:, C_REV:C_REV + NE]
                link(dve.tensor_reduce(rt(2), e1, AX.X, ALU.max))
                first_of(o1, e1, rt(2), rev, NE, rt(1))
                link(dve.scalar_tensor_tensor(e2, o1, -3.0 * BIG, e1, ALU.mult, ALU.add))
                link(dve.tensor_reduce(rt(3), e2, AX.X, ALU.max))
                first_of(o2, e2, rt(3), rev, NE, rt(1))
                dve.tensor_tensor(rt(4), rt(3), rt(2), ALU.subtract).then_inc(route_pre.sem, 1)
                dve.tensor_tensor(both[:, 0:nt, :], o1, o2, ALU.add).then_inc(choices_ready.sem, 1)
                dve.wait_ge(*route_exp.at(L, 1))
                link(dve.tensor_reduce(rt(6), grp[:, 2, 0:nt, :], AX.X, ALU.add))
                link(dve.tensor_scalar(rt(7), rt(5), 1.0, None, ALU.add))
                link(dve.tensor_tensor(rt(6), rt(6), rt(7), ALU.mult))
                link(dve.reciprocal(rt(8), rt(6)))
                link(dve.tensor_tensor(rt(9), rt(8), rt(5), ALU.mult))
                dve.wait_ge(*ranks_done.at(L, 1))
                rk, bk = rank[:, 0:nt, :], nbk[:, 0:nt, :]
                dve.tensor_copy(rk, ps[:, 4, R0:R0 + nt * NE].rearrange("p (t n) -> p t n", t=nt))
                link(dve.tensor_copy(cnt[:, 0, :], ps[:, 4, R0 + nt * NE:R0 + (nt + 1) * NE]))
                dve.tensor_scalar(bk, rk, float(rows), None, ALU.is_ge)
                link(dve.tensor_scalar(cnt[:, 1, :], cnt[:, 0, :], float(rows), None, ALU.is_gt))
                for b in range(2, nt * P // rows):
                    dve.scalar_tensor_tensor(bk, rk, float(b * rows), bk, ALU.is_ge, ALU.add)
                    link(dve.scalar_tensor_tensor(cnt[:, 1, :], cnt[:, 0, :], float(b * rows), cnt[:, 1, :],
                                                  ALU.is_gt, ALU.add))
                link(dve.tensor_tensor_scan(cnt[:, 2, :], ones[:, 0:NE], cnt[:, 1, :], 0.0, ALU.mult, ALU.add))
                link(dve.tensor_tensor(cnt[:, 3, :], cnt[:, 2, :], cnt[:, 1, :], ALU.subtract))
                link(dve.scalar_tensor_tensor(rk, bk, -float(rows), rk, ALU.mult, ALU.add))
                ew = [P, nt, NE]
                iot = cst[:, C_I32:C_I32 + NE].unsqueeze(1).broadcast_to(ew)
                tw = tmpe[:, 0:nt, :]
                link(dve.scalar_tensor_tensor(tw, bk, float(NE - 1), cnt[:, 3, :].unsqueeze(1).broadcast_to(ew),
                                              ALU.add, ALU.add))
                link(dve.tensor_tensor(tw, tw, iot, ALU.subtract))
                link(dve.scalar_tensor_tensor(tw, bk, 0.0, tw, ALU.is_gt, ALU.mult))
                link(dve.tensor_tensor(bk, tw, iot, ALU.add))
                for c_ in range(2):
                    for j, src in enumerate((rk, bk)):
                        link(dve.tensor_tensor(tw, oh[:, c_, 0:nt, :], src, ALU.mult))
                        link(dve.tensor_reduce(rowblk[:, j, c_, 0:nt], tw, AX.X, ALU.add))
                for c_ in range(2):
                    link(dve.scalar_tensor_tensor(slotf[:, c_, 0:nt], rowblk[:, 0, c_, 0:nt], float(NB),
                                                  rowblk[:, 1, c_, 0:nt], ALU.mult, ALU.add))
                    link(dve.tensor_copy(tokslot[:, c_, 0:nt], slotf[:, c_, 0:nt]))
                for i in range(nt):
                    for c_ in range(2):
                        j = 2 * i + c_
                        dve.tensor_scalar(ohrow[:, j, :], cst[:, C_I64:C_I64 + CAP], rowblk[:, 0, c_, i:i + 1], None,
                                          ALU.is_equal)
                        ins = dve.tensor_scalar(ohblk[:, j, :], cst[:, C_INB:C_INB + NB], rowblk[:, 1, c_, i:i + 1],
                                                cst[:, C_TOK + i:C_TOK + i + 1], ALU.is_equal, ALU.mult)
                ins.then_inc(table_operands_ready.sem, 1)
                ow = [P, OVER, NE]
                link(dve.tensor_tensor(ovf, cst[:, C_I32:C_I32 + OVER].unsqueeze(2).broadcast_to(ow),
                                       cnt[:, 2, :].unsqueeze(1).broadcast_to(ow), ALU.is_ge))
                link(dve.tensor_reduce(ovn[:, 0:OVER], ovf, AX.X, ALU.add))
                link(dve.tensor_copy(ovn[:, OVER:OVER + 1], cnt[:, 2, NE - 1:NE]))
                link(dve.tensor_copy(numi[:], ovn))
                dve.wait_ge(*table_done.at(L, 1))
                link(dve.tensor_scalar(idxf[0:CAP, 0, :], ps[0:CAP, 4, T0:T0 + NB], 0.0, 1e6, ALU.is_equal, ALU.mult))
                link(dve.scalar_tensor_tensor(idxf[0:CAP, 1, :], ps[0:CAP, 4, T0:T0 + NB], -1.0, idxf[0:CAP, 0, :],
                                              ALU.add, ALU.add))
                dve.tensor_copy(idx[0:CAP, :], idxf[0:CAP, 1, :]).then_inc(routed.sem, 1)
                if L < DEPTH - 1:
                    add_bias(L + 1, (0,))
                    add_bias(L + 1, (1, 2))

                def expert(X, b, par, early):
                    dve.wait_ge(*X.at("xg_turned", b + 1))
                    if early >= 2:
                        dve.wait_ge(*X.at("up_done", b - 1))
                    turned = ps[:, 0, :].rearrange("p (k n) -> p k n", k=KD)[:, :, 0:rows]
                    dve.tensor_copy(xgT[:, par, :, 0:rows], turned).then_inc(X.sem("xgT_ready"), 1)
                    dve.wait_ge(*X.at("silu_ready", b + 1))
                    if early >= 2:
                        dve.wait_ge(*X.at("h_turned", b - 1))
                    dve.tensor_tensor(hid[:, par, :], sg[:, par, :], ps[:, 1 + par, DE // 2:DE], ALU.mult).then_inc(X.sem("h_ready"), 1)
                    dve.wait_ge(*X.at("h_turned", b + 1))
                    if early >= 2:
                        dve.wait_ge(*X.at("down_done", b - 1))
                    dve.tensor_copy(hT[:, par].rearrange("p j n -> p (j n)"), ps[:, 3, 0:256]).then_inc(X.sem("hT_ready"), 1)

                for par in range(2):
                    expert(main[L], par, par, par)
                with dve.Fori(1, PAIRS) as i:
                    for par in range(2):
                        expert(main[L], 2 * i + par, par, 2)
                dve.wait_ge(*routed.at(L, 1))
                n_over = dve.value_load(numi[0:1, OVER:OVER + 1], min_val=0, max_val=OVER)
                with dve.If(n_over > 0):
                    with dve.Fori(0, n_over) as j:
                        expert(over[L], j, 0, 0)

                if L < DEPTH - 1:
                    norm_factors(L + 1, list(range(NT)), mod1_in)
                dve.wait_ge(*gate2_in.at(L, 32))
                for i, t in enumerate(tiles):
                    a, b = yg[:, i, 0, :], yg[:, i, 1, :]
                    dve.wait_ge(*y_gathered[i].at(L, 32))
                    dve.wait_ge(*y_scaled.at(L, i + 1))
                    link(dve.scalar_tensor_tensor(a, b, one[:, 9, i:i + 1], a, ALU.mult, ALU.add))
                    link(dve.tensor_tensor(a, a, g2b[:, stream(t), :], ALU.mult))
                    dve.tensor_tensor(h[:, t, :], h[:, t, :], a, ALU.add).then_inc(y_used.sem, 1)
                dve.wait_ge(*y_used.at(L, nt))

            norm_scale(2 * DEPTH)
            dve.wait_ge(fin_in, 16)
            for i, t in enumerate(range(LAT0, NT)):
                dve.scalar_tensor_tensor(xn[0][i], h[:, t, :], stat[:, 2 * DEPTH, 3, t:t + 1], gbc,
                                         ALU.mult, ALU.mult).then_inc(nrm[2 * DEPTH].sem("ready"), 1)

        @block.gpsimd
        def _(pool):
            counted = [0]

            def link(ins):
                counted[0] += 1
                ins.then_inc(pool_step, 1)
                pool.wait_ge(pool_step, counted[0])

            def row(ap):
                return ap.partition_broadcast(P)

            def load_bias(L):
                for m in range(4):
                    for st in range(2):
                        src = b_ada[L].rearrange("(n m c) -> m n c", n=12, m=4)[m:m + 1]
                        pool.dma_start(modR[32 * m + st:32 * m + st + 1], src).then_inc(layer_rows_in.sem, 16)

            def store_modulation(L, slices, ready):
                pool.wait_ge(*mod_rows_ready.at(L, ready))
                for m in range(4):
                    dst = mod_dram[L].rearrange("s (n m c) -> m s n c", n=12, m=4)[m]
                    pool.dma_start(dst[:, slices], modR[32 * m:32 * m + 2, slices]).then_inc(mod_stored.sem, 16)

            def load_norm1_rows(L, stored):
                pool.dma_start(gbc, row(norm1_g[L])).then_inc(mod1_in.sem, 16)
                pool.wait_ge(*mod_stored.at(L, stored))
                for st in range(2):
                    pool.dma_start(ab[:, st, 0, :], row(mod_dram[L, st, D:2 * D])).then_inc(mod1_in.sem, 16)
                    pool.dma_start(ab[:, st, 1, :], row(mod_dram[L, st, 0:D])).then_inc(mod1_in.sem, 16)

            for L in range(DEPTH):
                tiles = tiles_of(L)
                nt = len(tiles)
                rows = block_rows(L)
                if L == 0:
                    load_bias(0)
                    store_modulation(0, slice(0, 4), 1)
                    load_norm1_rows(0, 64)
                pool.wait_ge(*nrm[2 * L].at("ready", NT))
                pool.dma_start(ng, row(hgrn_norm_g[L])).then_inc(gain_rows_in.sem, 16)
                pool.dma_start(qkg[:, 0, :], row(q_norm_g[L])).then_inc(gain_rows_in.sem, 16)
                pool.dma_start(qkg[:, 1, :], row(k_norm_g[L])).then_inc(gain_rows_in.sem, 16)

                if L == 0:
                    pool.memset(zeros, 0.0).then_inc(zeros_ready, 1)
                    pool.wait_ge(zeros_ready, 1)
                    pool.dma_start(y_dram[:, NE:, :],
                                   zeros[0:CAP, :].unsqueeze(1).broadcast_to([CAP, OVER, D])).then_inc(y_cleared, 16)
                    store_modulation(0, slice(4, 12), 2)
                    pool.wait_ge(*mod_stored.at(0, 128))

                pool.wait_ge(*gain_rows_in.at(L, 48))
                pool.wait_ge(*projection_evacuated.at(L, 12 + NT + 2 * nt + NT))
                for t in range(NT):
                    for src, n, c0 in ((bq, B_HEADS, 0), (bkv, B_KV, B_HEADS)):
                        if src is bq and t not in tiles:
                            link(pool.memset(qst[:, 0, t * 10:t * 10 + B_HEADS], 1.0))
                            continue
                        a = src[:, t, 0:n * HD]
                        link(pool.tensor_tensor(qsq[:, 0:n * HD], a, a, ALU.mult))
                        s3 = qsq[:, 0:n * HD].rearrange("p (h n) -> p h n", h=n)
                        wd = HD // 2
                        while wd > 1:
                            link(pool.tensor_tensor(s3[:, :, 0:wd], s3[:, :, 0:wd], s3[:, :, wd:2 * wd], ALU.add))
                            wd //= 2
                        link(pool.tensor_tensor(qst[:, 0, t * 10 + c0:t * 10 + c0 + n].unsqueeze(2), s3[:, :, 0:1],
                                                s3[:, :, 1:2], ALU.add))
                pool.tensor_scalar(qst[:, 1, :], qst[:, 0, :], 1.0 / HD, EPS, ALU.mult, ALU.add).then_inc(qk_mean.sem, 1)
                pool.wait_ge(*qk_inverse_ready.at(L, 1))
                for t in range(NT):
                    for which, (src, n, c0) in enumerate(((bq, B_HEADS, 0), (bkv, B_KV, B_HEADS))):
                        if src is bq and t not in tiles:
                            continue
                        a = src[:, t, 0:n * HD].rearrange("p (h n) -> p h n", h=n)
                        w = [P, n, HD]
                        r = qst[:, 3, t * 10 + c0:t * 10 + c0 + n]
                        link(pool.tensor_tensor(a, a, r.unsqueeze(2).broadcast_to(w), ALU.mult))
                        link(pool.tensor_tensor(a, a, qkg[:, which, :].unsqueeze(1).broadcast_to(w), ALU.mult))
                        if t >= LAT0:
                            o = HD * (t - LAT0)
                            cs = cst[:, C_COS + o:C_COS + o + HD].unsqueeze(1).broadcast_to(w)
                            s3 = qsq[:, 0:n * HD].rearrange("p (h n) -> p h n", h=n)
                            for hf in range(2):
                                for ax in range(2):
                                    c1 = AXIS * ax + hf * AXIS // 2
                                    c2 = AXIS * ax + (1 - hf) * AXIS // 2
                                    sn = cst[:, C_SIN + o + c1:C_SIN + o + c1 + AXIS // 2].unsqueeze(1)
                                    sn = sn.broadcast_to([P, n, AXIS // 2])
                                    ins = pool.tensor_tensor(s3[:, :, c1:c1 + AXIS // 2], a[:, :, c2:c2 + AXIS // 2], sn, ALU.mult)
                            link(ins)
                            link(pool.tensor_tensor(a, a, cs, ALU.mult))
                            link(pool.tensor_tensor(a, a, s3, ALU.add))
                pool.memset(qst[:, 0, 0:1], 0.0).then_inc(qk_ready.sem, 1)

                pool.wait_ge(*mix_done.at(L, nt))
                for st in range(2):
                    pool.dma_start(g1b[:, st, :], row(mod_dram[L, st, 2 * D:3 * D])).then_inc(gate1_in.sem, 16)
                pool.wait_ge(*attn_turned.at(L, nt))
                for st in range(2):
                    pool.dma_start(ab[:, st, 0, :], row(mod_dram[L, st, 4 * D:5 * D])).then_inc(mod2_in.sem, 16)
                    pool.dma_start(ab[:, st, 1, :], row(mod_dram[L, st, 3 * D:4 * D])).then_inc(mod2_in.sem, 16)
                pool.wait_ge(*branch_done.at(L, KD))
                pool.dma_start(gbc, row(norm2_g[L])).then_inc(mod2_in.sem, 16)
                pool.dma_start(wr[:, :, 0:NG], w_rg[L].rearrange("(k p) n -> p k n", p=P)).then_inc(router_in.sem, 16)
                pool.dma_start(wr[:, :, NG:], w_re[L].rearrange("(k p) n -> p k n", p=P)).then_inc(router_in.sem, 16)
                pool.dma_start(rb[:, 0:NG], row(b_rg[L])).then_inc(router_in.sem, 16)
                pool.dma_start(rb[:, NG:], row(b_re[L])).then_inc(router_in.sem, 16)
                for i, t in enumerate(tiles):
                    pool.wait_ge(*nrm[2 * L + 1].at("ready", i + 1))
                    pool.dma_start(xs_dram[L][tk(i), :], xn[1][i]).then_inc(moe_input_stored[i % 2].sem, 16)
                for st in range(2):
                    pool.dma_start(g2b[:, st, :], row(mod_dram[L, st, 5 * D:6 * D])).then_inc(gate2_in.sem, 16)
                if L == DEPTH - 1:
                    pool.dma_start(gbc, row(final_norm_g)).then_inc(fin_in, 16)
                if L < DEPTH - 1:
                    load_bias(L + 1)
                for one_of in moe_input_stored:
                    pool.wait_ge(*one_of.at(L, 8 * nt))
                pool.wait_ge(*nrm[2 * L + 1].at("turned", nt))
                pool.memset(xg[:], 0.0).then_inc(xg_clear, 1)
                pool.wait_ge(xg_clear, L + 1)
                pool.wait_ge(*routed.at(L, 1))

                def expert(X, b, i, par, early, column):
                    if early >= 2:
                        pool.wait_ge(*X.at("xg_turned", b - 1))
                    pool.tensor_copy(idxc[0:rows, par:par + 1], idx[0:rows, column]).then_inc(X.sem("idx_ready"), 1)
                    pool.wait_ge(*X.at("idx_ready", b + 1))
                    alone(pool)
                    pool.indirect_dma_start(xg[0:rows, par, :], None, xs_dram[L],
                                            bass.IndirectOffsetOnAxis(ap=idxc[0:rows, par:par + 1], axis=0),
                                            bounds_check=nt * P - 1, oob_is_err=False).then_inc(X.sem(f"xg_in{par}"), 16)

                for par in range(2):
                    expert(main[L], par, 0, par, par, slice(par, par + 1))
                if L < DEPTH - 1:
                    store_modulation(L + 1, slice(0, 4), 2)
                    store_modulation(L + 1, slice(4, 12), 2)
                with pool.Fori(1, PAIRS) as i:
                    for par in range(2):
                        expert(main[L], 2 * i + par, i, par, 2, bass.ds(2 * i + par, 1))
                if L < DEPTH - 1:
                    load_norm1_rows(L + 1, 128)
                pool.wait_ge(*main[L].at("y_stored0", 32 * PAIRS))
                pool.wait_ge(*main[L].at("y_stored1", 32 * PAIRS))
                n_over = pool.value_load(numi[0:1, OVER:OVER + 1], min_val=0, max_val=OVER)
                with pool.If(n_over > 0):
                    with pool.Fori(0, n_over) as j:
                        expert(over[L], j, j, 0, 0, bass.ds(j + NE, 1))
                        pool.wait_ge(*over[L].at("y_stored0", 32 * j + 32))
                for i, t in enumerate(tiles):
                    for c_ in range(2):
                        pool.indirect_dma_start(yg[:, i, c_, :], None, y_rows,
                                                bass.IndirectOffsetOnAxis(ap=tokslot[:, c_, i:i + 1], axis=0),
                                                bounds_check=CAP * NB - 1, oob_is_err=False).then_inc(y_gathered[i].sem, 16)


INS = ["x", "c", "ctx", "c_ctx", "w_ada", "b_ada", "norm1_g", "norm2_g", "w_in", "lb_logits", "hgrn_norm_g",
       "q_norm_g", "k_norm_g", "w_up_a", "w_up_b", "w_out", "w_router_group", "b_router_group", "w_router_expert",
       "b_router_expert", "w_gate", "w_up", "w_down", "final_norm_g"]


def kernel(**inputs):
    import concourse.bacc as bacc
    from concourse.bass_utils import run_bass_kernel_spmd

    nc = bacc.Bacc("TRN2", target_bir_lowering=False, num_devices=1)
    arrays, args = {}, []
    for name in INS:
        a = np.ascontiguousarray(inputs[name])
        arrays[f"in_{name}"] = a
        args.append(nc.dram_tensor(f"in_{name}", a.shape, mybir.dt.from_np(a.dtype), kind="ExternalInput").ap())
    for name, a in (("consts", float_constants()), ("masks", level_masks())):
        arrays[f"in_{name}"] = a
        args.append(nc.dram_tensor(f"in_{name}", a.shape, mybir.dt.from_np(a.dtype), kind="ExternalInput").ap())
    out = nc.dram_tensor("out", (1, SEQ, D), F32, kind="ExternalOutput").ap()
    program(nc, *args, out)
    r = run_bass_kernel_spmd(nc, [arrays], core_ids=[0])
    return r.results[0]["out"]
```
